# Optimizing a Trainium2 kernel written in Bass

```python
import math
import jax, jax.numpy as jnp
from jax import lax
import numpy as np

D_MODEL = 2048
BATCH = 1
SEQ = 256
DEPTH = 2
DEC_BATCH = 8
DEC_SEQ = 1
PAST_LEN = 2048
PAGE_SIZE = 128

N_A_LAYERS = DEPTH // 2
N_B_LAYERS = DEPTH - N_A_LAYERS
DN_HEAD_DIM = 128
DN_QK_HEADS = D_MODEL // 128
DN_V_HEADS = 2 * DN_QK_HEADS
DN_KEY_DIM = DN_QK_HEADS * DN_HEAD_DIM
DN_VAL_DIM = DN_V_HEADS * DN_HEAD_DIM
DN_CONV_DIM = 2 * DN_KEY_DIM + DN_VAL_DIM
DN_CONV_W = 4
DN_CHUNK = 64
DN_IN_DIM = DN_CONV_DIM + DN_VAL_DIM + 2 * DN_V_HEADS
SWA_HEAD_DIM = 64
SWA_HEADS = D_MODEL // SWA_HEAD_DIM
SWA_KV_HEADS = SWA_HEADS // 8
SWA_GROUP = SWA_HEADS // SWA_KV_HEADS
SWA_Q_DIM = SWA_HEADS * SWA_HEAD_DIM
SWA_KV_DIM = SWA_KV_HEADS * SWA_HEAD_DIM
WINDOW = 128
ATTN_SCALE = SWA_HEAD_DIM ** -0.5
REL_BUCKETS = 32
REL_MAX_DIST = 128
D_FF = -(-8 * D_MODEL // (3 * 256)) * 256
EPS = 1e-6

kernel_name = 'yoco_gated_deltanet_swa_sink_step'

def rms_norm(x, g):
    x32 = x.astype(jnp.float32)
    y = x32 * lax.rsqrt(jnp.mean(x32 * x32, axis=-1, keepdims=True) + EPS)
    return (y * g.astype(jnp.float32)).astype(x.dtype)

def l2_normalize(x):
    x32 = x.astype(jnp.float32)
    return x32 * lax.rsqrt(jnp.sum(x32 * x32, axis=-1, keepdims=True) + EPS)

def swiglu_ffn(h, w_gate_up, w_down):
    gate, up = jnp.split(h @ w_gate_up, 2, axis=-1)
    return (jax.nn.silu(gate) * up) @ w_down

def gated_delta_chunked(q, k, v, g, beta):
    B, L, H, dk = q.shape
    dv = v.shape[-1]
    C = DN_CHUNK
    N = L // C
    def to_chunks(t):
        return jnp.moveaxis(t.reshape((B, N, C, H) + t.shape[3:]), 3, 1)
    q, k, v, g, beta = (to_chunks(t) for t in (q, k, v, g, beta))
    gc = jnp.cumsum(g, axis=-1)
    idx = jnp.arange(C)
    incl = idx[:, None] >= idx[None, :]
    strict = idx[:, None] > idx[None, :]
    diff = gc[..., :, None] - gc[..., None, :]
    decay = jnp.where(incl, jnp.exp(jnp.where(incl, diff, 0.0)), 0.0)
    kb = k * beta[..., None]
    a_mat = jnp.where(strict, jnp.einsum('bhnid,bhnjd->bhnij', kb, k) * decay, 0.0)
    eye = jnp.eye(C, dtype=jnp.float32)
    t_mat = lax.linalg.triangular_solve(a_mat + eye, jnp.broadcast_to(eye, a_mat.shape),
                                        left_side=True, lower=True)
    u = t_mat @ (v * beta[..., None])
    w = t_mat @ (kb * jnp.exp(gc)[..., None])
    intra = jnp.einsum('bhnid,bhnjd->bhnij', q, k) * decay
    g_last = gc[..., -1]
    q_dec = q * jnp.exp(gc)[..., None]
    k_dec = k * jnp.exp(g_last[..., None] - gc)[..., None]

    def chunk_step(S, xs):
        u_n, w_n, q_n, intra_n, k_n, gl_n = xs
        v_new = u_n - w_n @ S
        o_n = q_n @ S + intra_n @ v_new
        S = S * jnp.exp(gl_n)[..., None, None] + jnp.einsum('bhcd,bhce->bhde', k_n, v_new)
        return S, o_n

    xs = tuple(jnp.moveaxis(t, 2, 0) for t in (u, w, q_dec, intra, k_dec, g_last))
    S0 = jnp.zeros((B, H, dk, dv), jnp.float32)
    S, o = lax.scan(chunk_step, S0, xs)
    o = jnp.moveaxis(o, 0, 2).reshape(B, H, L, dv).transpose(0, 2, 1, 3)
    return o, S

def gated_delta_recurrent(q, k, v, g, beta, S0):
    def token_step(S, xs):
        q_t, k_t, v_t, g_t, b_t = xs
        S = S * jnp.exp(g_t)[..., None, None]
        kv_mem = jnp.einsum('bhde,bhd->bhe', S, k_t)
        S = S + jnp.einsum('bhd,bhe->bhde', k_t, (v_t - kv_mem) * b_t[..., None])
        return S, jnp.einsum('bhde,bhd->bhe', S, q_t)
    xs = tuple(jnp.moveaxis(t, 1, 0) for t in (q, k, v, g, beta))
    S, o = lax.scan(token_step, S0, xs)
    return jnp.moveaxis(o, 0, 1), S

def deltanet_mixer(h, conv_prev, S0, w_in, conv_w, a_log, dt_bias, gnorm, w_out):
    B, L, _ = h.shape
    proj = h @ w_in
    o1 = DN_CONV_DIM
    o2 = o1 + DN_VAL_DIM
    o3 = o2 + DN_V_HEADS
    qkv_raw, z, b_raw, a_raw = proj[..., :o1], proj[..., o1:o2], proj[..., o2:o3], proj[..., o3:]
    if conv_prev is None:
        prev = jnp.zeros((B, DN_CONV_W - 1, DN_CONV_DIM), qkv_raw.dtype)
    else:
        prev = conv_prev.astype(qkv_raw.dtype)
    x_ext = jnp.concatenate([prev, qkv_raw], axis=1)
    conv = x_ext[:, 0:L] * conv_w[0]
    for j in range(1, DN_CONV_W):
        conv = conv + x_ext[:, j:j + L] * conv_w[j]
    qkv = jax.nn.silu(conv)
    rep = DN_V_HEADS // DN_QK_HEADS
    q = qkv[..., :DN_KEY_DIM].reshape(B, L, DN_QK_HEADS, DN_HEAD_DIM)
    k = qkv[..., DN_KEY_DIM:2 * DN_KEY_DIM].reshape(B, L, DN_QK_HEADS, DN_HEAD_DIM)
    v = qkv[..., 2 * DN_KEY_DIM:].reshape(B, L, DN_V_HEADS, DN_HEAD_DIM).astype(jnp.float32)
    q = jnp.repeat(l2_normalize(q) * DN_HEAD_DIM ** -0.5, rep, axis=2)
    k = jnp.repeat(l2_normalize(k), rep, axis=2)
    beta = jax.nn.sigmoid(b_raw.astype(jnp.float32))
    g = -jnp.exp(a_log.astype(jnp.float32)) * jax.nn.softplus(a_raw.astype(jnp.float32) + dt_bias.astype(jnp.float32))
    if S0 is None:
        o, S = gated_delta_chunked(q, k, v, g, beta)
    else:
        o, S = gated_delta_recurrent(q, k, v, g, beta, S0.astype(jnp.float32))
    z = z.reshape(B, L, DN_V_HEADS, DN_HEAD_DIM).astype(jnp.float32)
    o = rms_norm(o, gnorm) * jax.nn.silu(z)
    y = o.astype(h.dtype).reshape(B, L, DN_VAL_DIM) @ w_out
    return y, x_ext[:, -(DN_CONV_W - 1):], S

def t5_bucket(dist):
    d = jnp.maximum(dist, 0)
    max_exact = REL_BUCKETS // 2
    large = max_exact + (jnp.log(jnp.maximum(d, max_exact).astype(jnp.float32) / max_exact)
                         / math.log(REL_MAX_DIST / max_exact)
                         * (REL_BUCKETS - max_exact)).astype(jnp.int32)
    return jnp.where(d < max_exact, d, jnp.minimum(large, REL_BUCKETS - 1))

def sink_attention(q, k, v, dist, valid, rel_bias, sinks):
    s = jnp.einsum('...qkgd,...ckd->...kgqc', q, k, preferred_element_type=jnp.float32) * ATTN_SCALE
    bias = jnp.moveaxis(rel_bias[t5_bucket(dist)], -1, 0).reshape((SWA_KV_HEADS, SWA_GROUP) + dist.shape)
    s = jnp.where(valid, s + bias.astype(jnp.float32), -jnp.inf)
    sink = sinks.astype(jnp.float32).reshape(SWA_KV_HEADS, SWA_GROUP)[:, :, None, None]
    m = jnp.maximum(jnp.max(s, axis=-1, keepdims=True), sink)
    p = jnp.exp(s - m)
    p = p / (jnp.sum(p, axis=-1, keepdims=True) + jnp.exp(sink - m))
    return jnp.einsum('...kgqc,...ckd->...qkgd', p.astype(v.dtype), v)

def swa_prompt(q, k, v, rel_bias, sinks):
    B, L = q.shape[:2]
    nb = L // WINDOW
    qb = q.reshape(B, nb, WINDOW, SWA_KV_HEADS, SWA_GROUP, SWA_HEAD_DIM)
    pad = ((0, 0), (WINDOW, 0), (0, 0), (0, 0))
    kp = jnp.pad(k, pad).reshape(B, nb + 1, WINDOW, SWA_KV_HEADS, SWA_HEAD_DIM)
    vp = jnp.pad(v, pad).reshape(B, nb + 1, WINDOW, SWA_KV_HEADS, SWA_HEAD_DIM)
    kb = jnp.concatenate([kp[:, :-1], kp[:, 1:]], axis=2)
    vb = jnp.concatenate([vp[:, :-1], vp[:, 1:]], axis=2)
    qi = jnp.arange(WINDOW)[:, None]
    ci = jnp.arange(2 * WINDOW)[None, :]
    dist = qi + WINDOW - ci
    key_pos = jnp.arange(nb)[:, None, None] * WINDOW - WINDOW + ci
    valid = (dist >= 0) & (dist < WINDOW) & (key_pos >= 0)
    o = sink_attention(qb, kb, vb, dist, valid[:, None, None], rel_bias, sinks)
    return o.reshape(B, L, SWA_Q_DIM)

def swa_sample(q, k_all, v_all, rel_bias, sinks):
    B, T = q.shape[:2]
    Tk = k_all.shape[1]
    qi = jnp.arange(T)[:, None]
    ci = jnp.arange(Tk)[None, :]
    dist = qi + (Tk - T) - ci
    valid = (dist >= 0) & (dist < WINDOW)
    o = sink_attention(q, k_all, v_all, dist, valid, rel_bias, sinks)
    return o.reshape(B, T, SWA_Q_DIM)

def trunk(x, prompt, state_delta, state_conv, cache_k_win, cache_v_win,
          norm_mix, norm_ffn, w_in_a, conv_w_a, a_log, dt_bias, gnorm_a, w_out_a,
          norm_kv, w_kv, w_q_b, w_o_b, sinks, rel_bias, w_gate_up, w_down, norm_final):
    B, L, _ = x.shape
    new_delta, new_conv = [], []
    for i in range(N_A_LAYERS):
        h = rms_norm(x, norm_mix[i])
        y, conv_buf, S = deltanet_mixer(h, None if prompt else state_conv[i],
                                        None if prompt else state_delta[i],
                                        w_in_a[i], conv_w_a[i], a_log[i], dt_bias[i],
                                        gnorm_a[i], w_out_a[i])
        x = x + y
        x = x + swiglu_ffn(rms_norm(x, norm_ffn[i]), w_gate_up[i], w_down[i])
        new_delta.append(S)
        new_conv.append(conv_buf)
    kv = rms_norm(x, norm_kv) @ w_kv
    k_new = kv[..., :SWA_KV_DIM].reshape(B, L, SWA_KV_HEADS, SWA_HEAD_DIM)
    v_new = kv[..., SWA_KV_DIM:].reshape(B, L, SWA_KV_HEADS, SWA_HEAD_DIM)
    if prompt:
        k_all, v_all = k_new, v_new
    else:
        k_all = jnp.concatenate([cache_k_win.astype(k_new.dtype), k_new], axis=1)
        v_all = jnp.concatenate([cache_v_win.astype(v_new.dtype), v_new], axis=1)
    for j in range(N_B_LAYERS):
        i = N_A_LAYERS + j
        h = rms_norm(x, norm_mix[i])
        q = (h @ w_q_b[j]).reshape(B, L, SWA_KV_HEADS, SWA_GROUP, SWA_HEAD_DIM)
        if prompt:
            o = swa_prompt(q, k_all, v_all, rel_bias, sinks[j])
        else:
            o = swa_sample(q, k_all, v_all, rel_bias, sinks[j])
        x = x + o @ w_o_b[j]
        x = x + swiglu_ffn(rms_norm(x, norm_ffn[i]), w_gate_up[i], w_down[i])
    y = rms_norm(x, norm_final)
    return y, jnp.stack(new_delta), jnp.stack(new_conv), k_all[:, -WINDOW:], v_all[:, -WINDOW:]

def setup_inputs(seed: int = 0) -> dict:
    key = jax.random.key(seed)
    ks = jax.random.split(key, 24)
    def nrm(k, shape, scale):
        return jax.random.normal(k, shape, jnp.float32) * scale
    D = D_MODEL
    dt = jnp.exp(jax.random.uniform(ks[11], (N_A_LAYERS, DN_V_HEADS), jnp.float32,
                                    minval=math.log(1e-3), maxval=math.log(1e-1)))
    return {
        'x_prompt': nrm(ks[0], (BATCH, SEQ, D), 1.0),
        'x_sample': nrm(ks[1], (DEC_BATCH, DEC_SEQ, D), 1.0),
        'state_delta': nrm(ks[2], (N_A_LAYERS, DEC_BATCH, DN_V_HEADS, DN_HEAD_DIM, DN_HEAD_DIM), 0.05),
        'state_conv': nrm(ks[3], (N_A_LAYERS, DEC_BATCH, DN_CONV_W - 1, DN_CONV_DIM), 1.0),
        'cache_k_win': nrm(ks[4], (DEC_BATCH, WINDOW, SWA_KV_HEADS, SWA_HEAD_DIM), 1.0),
        'cache_v_win': nrm(ks[5], (DEC_BATCH, WINDOW, SWA_KV_HEADS, SWA_HEAD_DIM), 1.0),
        'norm_mix': 1.0 + nrm(ks[6], (DEPTH, D), 0.05),
        'norm_ffn': 1.0 + nrm(ks[7], (DEPTH, D), 0.05),
        'w_in_a': nrm(ks[8], (N_A_LAYERS, D, DN_IN_DIM), D ** -0.5),
        'conv_w_a': nrm(ks[9], (N_A_LAYERS, DN_CONV_W, DN_CONV_DIM), DN_CONV_W ** -0.5),
        'a_log': jnp.log(jax.random.uniform(ks[10], (N_A_LAYERS, DN_V_HEADS), jnp.float32, minval=1.0, maxval=16.0)),
        'dt_bias': dt + jnp.log(-jnp.expm1(-dt)),
        'gnorm_a': 1.0 + nrm(ks[12], (N_A_LAYERS, DN_HEAD_DIM), 0.05),
        'w_out_a': nrm(ks[13], (N_A_LAYERS, DN_VAL_DIM, D), DN_VAL_DIM ** -0.5),
        'norm_kv': 1.0 + nrm(ks[14], (D,), 0.05),
        'w_kv': nrm(ks[15], (D, 2 * SWA_KV_DIM), D ** -0.5),
        'w_q_b': nrm(ks[16], (N_B_LAYERS, D, SWA_Q_DIM), D ** -0.5),
        'w_o_b': nrm(ks[17], (N_B_LAYERS, SWA_Q_DIM, D), SWA_Q_DIM ** -0.5),
        'sinks': nrm(ks[18], (N_B_LAYERS, SWA_HEADS), 0.5),
        'rel_bias': nrm(ks[19], (REL_BUCKETS, SWA_HEADS), 0.5),
        'w_gate_up': nrm(ks[20], (DEPTH, D, 2 * D_FF), D ** -0.5),
        'w_down': nrm(ks[21], (DEPTH, D_FF, D), D_FF ** -0.5),
        'norm_final': 1.0 + nrm(ks[22], (D,), 0.05),
    }

def reference(x_prompt, x_sample, state_delta, state_conv, cache_k_win, cache_v_win,
              norm_mix, norm_ffn, w_in_a, conv_w_a, a_log, dt_bias, gnorm_a, w_out_a,
              norm_kv, w_kv, w_q_b, w_o_b, sinks, rel_bias, w_gate_up, w_down, norm_final):
    y_prompt, delta_p, conv_p, k_win_p, v_win_p = trunk(
        x_prompt, True, None, None, None, None,
        norm_mix, norm_ffn, w_in_a, conv_w_a, a_log, dt_bias, gnorm_a, w_out_a,
        norm_kv, w_kv, w_q_b, w_o_b, sinks, rel_bias, w_gate_up, w_down, norm_final)
    y_sample, delta_s, conv_s, k_win_s, v_win_s = trunk(
        x_sample, False, state_delta, state_conv, cache_k_win, cache_v_win,
        norm_mix, norm_ffn, w_in_a, conv_w_a, a_log, dt_bias, gnorm_a, w_out_a,
        norm_kv, w_kv, w_q_b, w_o_b, sinks, rel_bias, w_gate_up, w_down, norm_final)
    return (y_prompt, y_sample, delta_p, conv_p, k_win_p, v_win_p, delta_s, conv_s, k_win_s, v_win_s)


_drawn_inputs = setup_inputs


def setup_inputs(seed=0):
    import zlib

    import numpy as np

    out = dict(_drawn_inputs(seed))
    spreads = {}
    factors = {'sinks': 6.522}
    for name, (base, spread) in spreads.items():
        noise = np.random.default_rng([zlib.crc32(name.encode()), seed]).standard_normal(out[name].shape)
        drawn = base * np.exp(spread * noise) if base else spread * noise
        out[name] = __import__('jax').numpy.asarray(drawn.astype(out[name].dtype))
    for name, factor in factors.items():
        out[name] = (out[name] * factor).astype(out[name].dtype)
    return out
```

```python
from contextlib import ExitStack

import concourse.bass as bass
import numpy as np
from concourse import mybir

ALU = mybir.AluOpType
ACT = mybir.ActivationFunctionType
AX = mybir.AxisListType
F32 = mybir.dt.float32
F32R = mybir.dt.float32r
ds = bass.ds

P = 128
EPS = 1e-6
CHUNK = 128
RAW = 4
ELEMS = 1024
WINDOW = 128
BUCKETS = 32
MASKED = -1e30
NCONST = 9
SEL = 8


def shape_constants():
    i = np.arange(P)
    row, col = i[:, None], i[None, :]
    up = row < col
    same = lambda m: row // m == col // m
    level = lambda m: same(2 * m) & ~same(m) & up
    blocks = [
        row == col, row <= col, up, up & same(16), (row > col) & same(16),
        level(16), level(32), level(64), row >= 0,
    ]
    c = np.concatenate([b.astype(np.float32) * np.ones((P, P), np.float32) for b in blocks], axis=1)
    dist = 2 * WINDOW - 1 - np.arange(3 * WINDOW)
    exact = BUCKETS // 2
    far = exact + (np.log(np.maximum(dist, exact).astype(np.float32) / exact)
                   / np.log(np.float32(WINDOW / exact)) * (BUCKETS - exact)).astype(np.int32)
    bucket = np.where(dist < exact, dist, np.minimum(far, BUCKETS - 1))
    valid = (dist >= 0) & (dist < WINDOW)
    onehot = ((bucket[None, :] == np.arange(BUCKETS)[:, None]) & valid).astype(np.float32)
    floor = np.where(valid, 0.0, MASKED).astype(np.float32)[None, :] * np.ones((BUCKETS, 1), np.float32)
    c = np.concatenate([c, (row % 32 == np.arange(SEL)[None, :]).astype(np.float32)], axis=1)
    return np.ascontiguousarray(c), np.ascontiguousarray(np.concatenate([onehot, floor], axis=1))


def yoco_step(nc, x_prompt, x_sample, state_delta, state_conv, cache_k, cache_v, norm_mix, norm_ffn,
              w_in, conv_w, a_log, dt_bias, gnorm, w_out, norm_kv, w_kv, w_q, w_o, sinks, rel_bias,
              w_gate_up, w_down, norm_final, masks_in, buckets_in,
              y_prompt, y_sample, delta_p, conv_p, kwin_p, vwin_p, delta_s, conv_s, kwin_s, vwin_s):
    D = x_prompt.shape[2]
    NP = x_prompt.shape[1]
    NB = x_sample.shape[0]
    T = NP + NB
    KT = D // P
    VH = state_delta.shape[2]
    GROUPS = VH // 2
    CT = conv_w.shape[2] // P
    FF = w_down.shape[1]
    FT = FF // P
    HEADS = sinks.shape[1]
    KV = cache_k.shape[2]
    HD = cache_k.shape[3]
    NBLK = NP // P
    QS = float(P) ** -0.5
    ATT = float(HD) ** -0.5
    assert NB == SEL and NP == 2 * CHUNK and VH == 32 and T * 4 <= 2048

    C_BA = 0
    C_IN = C_BA + 2
    C_OUT = C_IN + 12 * GROUPS
    UNIT = {"out": 2 * KT // 2, "q": KT // 2, "o": KT // 2, "gu": KT // 2, "down": FT // 2, "kv": KT // 2}
    C_GU = [0, 0]
    C_DOWN = [0, 0]
    C_GU[0] = C_OUT + 4 * UNIT["out"]
    C_DOWN[0] = C_GU[0] + (FT // 2) * UNIT["gu"]
    C_KV = C_DOWN[0] + 4 * UNIT["down"]
    C_Q = C_KV + UNIT["kv"]
    C_O = C_Q + 4 * UNIT["q"]
    C_GU[1] = C_O + 4 * UNIT["o"]
    C_DOWN[1] = C_GU[1] + (FT // 2) * UNIT["gu"]
    C_END = C_DOWN[1] + 4 * UNIT["down"]

    SPL = 2

    def chunk(base, per, g, j):
        a, s = divmod(base + j, RAW)
        return (per // RAW) * g + a, s

    x_spill = nc.dram_tensor("x_spill", [P, KT * T], F32, kind="Internal").ap()
    bias_rows = nc.dram_tensor("bias_rows", [HEADS, 3 * WINDOW], F32, kind="Internal").ap()
    bias_tiles = nc.dram_tensor("bias_tiles", [HEADS, P, 3 * WINDOW], F32, kind="Internal").ap()

    ctx = ExitStack()
    with ctx:
        def sb(name, shape, dt=F32, stack=ctx):
            return stack.enter_context(nc.sbuf_tensor(name, shape, dt))

        def sem(name):
            return ctx.enter_context(nc.semaphore(name))

        bank = [ctx.enter_context(nc.psum_tensor(f"bank{i}", [P, 512], F32)) for i in range(8)]
        B = bank[4:]

        masks = sb("masks", [P, NCONST * P + SEL])
        ident, incl, strict, base_up, base_lo, lvl16, lvl32, lvl64, ones = (
            masks[:, i * P:(i + 1) * P] for i in range(NCONST))
        sel8 = masks[:, NCONST * P:NCONST * P + NB]
        gains = sb("gains", [P, 6 * KT + 1])
        bias_c = sb("bias_c", [P, 2])
        h_hi = sb("h_hi", [P, KT, T], F32R)
        h_lo = sb("h_lo", [P, KT, T], F32R)
        w_raw = sb("w_raw", [P, RAW, ELEMS])
        w_hi = sb("w_hi", [P, SPL, ELEMS], F32R)
        w_lo = sb("w_lo", [P, SPL, ELEMS], F32R)
        rstd = sb("rstd", [P, T])
        norm_sq = sb("norm_sq", [P, 2, T])
        norm_h = sb("norm_h", [P, 2, T])

        dl = ExitStack()
        with dl:
            def sd(name, shape, dt=F32):
                return sb(name, shape, dt, dl)
            convw = sd("convw", [P, GROUPS, 4, 4])
            prevconv = sd("prevconv", [P, GROUPS, 4, NB])
            tab_gc = sd("tab_gc", [P, VH, 2])
            tab_beta = sd("tab_beta", [P, VH, 2])
            tab_neg = sd("tab_neg", [P, VH])
            row_eg = sd("row_eg", [P, VH, NB])
            tab_eb = sd("tab_eb", [P, VH, 3])
            gc_rows = sd("gc_rows", [VH, NP])
            setup = ExitStack()
            with setup:
                def su(name, shape, dt=F32):
                    return sb(name, shape, dt, setup)
                x_first = su("x_first", [P, KT, T])
                x_rows = su("x_rows", [P, NBLK, D])
                x_rows_d = su("x_rows_d", [NB, D])
                rows_in = su("rows_in", [P, 3, P])
                sc_rows = su("sc_rows", [3 * NB, CT * P])
                scT = su("scT", [P, CT, NB, 3])
                cw_n = su("cw_n", [P, 4, CT])
                pc_a = su("pc_a", [P, CT, NB])
                pc_b = su("pc_b", [P, CT, NB])
                ba = su("ba", [VH, 8, T])
                hcol = su("hcol", [VH, 4])
                tok_gb = su("tok_gb", [P, 2, 2, VH])
                dexp = su("dexp", [VH, VH, NB])
                gb_pad = su("gb_pad", [VH, 2, P])
                buckets = su("buckets", [BUCKETS, 6 * WINDOW])
                relb = su("relb", [BUCKETS, HEADS])
                brow = su("brow", [HEADS, 3 * WINDOW])
            tail = ExitStack()
            with tail:
                def st_(name, shape, dt=F32):
                    return sb(name, shape, dt, tail)
                o_hi = st_("o_hi", [P, 2 * KT, T], F32R)
                o_lo = st_("o_lo", [P, 2 * KT, T], F32R)
                craw = st_("craw", [P, 4, 3 + T])
                cacc = st_("cacc", [P, 4, T])
                qk = st_("qk", [P, 2, T])
                vv = st_("vv", [P, 2, T])
                zs = st_("zs", [P, 2, T])
                ktok = st_("ktok", [P, 2, P])
                vtok = st_("vtok", [P, 2, 2, P])
                ET = st_("ET", [P, 4, P])
                intraT = st_("intraT", [P, 4, P])
                Nm = st_("Nm", [P, 4, P])
                Pa = st_("Pa", [P, 4, P])
                PaT = st_("PaT", [P, 4, P])
                Pb = st_("Pb", [P, 4, P])
                PbT = st_("PbT", [P, 4, P])
                Um = st_("Um", [P, 4, P])
                egR = st_("egR", [P, 2, P])
                qdec = st_("qdec", [P, 2, P])
                vn = st_("vn", [P, 2, P])
                vn2 = st_("vn2", [P, 2, P])
                S1 = st_("S1", [P, 2, P])
                S2 = st_("S2", [P, 2, P])
                s_dec = st_("s_dec", [P, 2, NB, P])
                strow = st_("strow", [3 + NB, 4, P])
                kmask = st_("kmask", [96, NB, P], F32R)
                dec_dr = st_("dec_dr", [96, 2, P], F32R)
                kq_diag = st_("kq_diag", [P, NB * (P + 1)])
                kv_pad = st_("kv_pad", [P, 3, 96])
                dec_qk = st_("dec_qk", [P, NB])
                dec_sel = st_("dec_sel", [P, 2, NB])
                sc_g = st_("sc_g", [P, 4])
                sc_b = st_("sc_b", [P, 4])
                sc_n = st_("sc_n", [P, 2])
                sc_e = st_("sc_e", [P, 4])
                sc_eg = st_("sc_eg", [P, 2, NB])
                sc_eb = st_("sc_eb", [P, 2, 3])
                sqn, oT, Tm, NT, Xm, rhs = norm_sq, norm_h, ET, PbT, PbT, vn
                selh = Pa[0:VH, 1:3, :]
                dec_kd = Pa[0:96, 0, :].bitcast(F32R)
                dec_d = Pb[:, 0:2, :]

        low = ExitStack()
        with low:
            a_hi = sb("a_hi", [P, FT, T], F32R, low)
            a_lo = sb("a_lo", [P, FT, T], F32R, low)
            x_res = sb("x_res", [P, KT, T], F32, low)
            f_silu = sb("f_silu", [P, 2, T], F32, low)
            f_h = sb("f_h", [P, 2, T], F32, low)
            f_sq = sb("f_sq", [P, 4, T], F32, low)
            part = sb("part", [P, 4, T], F32, low)
        att = ExitStack()
        with att:
            def sa(name, shape, dt=F32):
                return sb(name, shape, dt, att)
            ao_hi = sa("ao_hi", [P, KT, T], F32R)
            ao_lo = sa("ao_lo", [P, KT, T], F32R)
            qT = sa("qT", [P, KT, T])
            kvT = sa("kvT", [P, 4, T])
            kdup = sa("kdup", [P, KV, NP])
            vtk = sa("vtk", [P, NBLK, KV, HD])
            newtok = sa("newtok", [NB, 2, KV * HD])
            ktw = sa("ktw", [P, KV * HD])
            sink_all = sa("sink_all", [P, HEADS])
            two = ExitStack()
            with two:
                def s2(name, shape, dt=F32):
                    return sb(name, shape, dt, two)
                q_st = s2("q_st", [P, 4, NP])
                k_st = s2("k_st", [P, NP])
                v_st = s2("v_st", [P, NBLK, HD])
                bias = s2("bias", [P, 8, 2 * WINDOW])
                sink_st = s2("sink_st", [P, 8])
                scores_sb = s2("scores", [P, 2, 2, 3 * WINDOW])
                smx = s2("smx", [P, 2, 4])
                snm = s2("snm", [P, 2, 4])
                ssum = s2("ssum", [P, 2, 4])
                ses = s2("ses", [P, 2, 4])
                srec = s2("srec", [P, 2, 4])
                pT = s2("pT", [P, 6, WINDOW])
                o_st = s2("o_st", [P, 4, NP])
            three = ExitStack()
            with three:
                def s3(name, shape, dt=F32):
                    return sb(name, shape, dt, three)
                k_win = s3("k_win", [P, NB, KV, HD])
                v_win = s3("v_win", [P, NB, KV, HD])
                k_t = s3("k_t", [P, 2, KV, P])
                bias_d = s3("bias_d", [P, WINDOW])
                sink_d = s3("sink_d", [P, 1])
                sT = s3("sT", [P, NB * HEADS // 2, 2])
                sdc = s3("sdc", [P, 2, WINDOW])
                dmx = s3("dmx", [P, 2])
                dnm = s3("dnm", [P, 2])
                dsum = s3("dsum", [P, 2])
                des = s3("des", [P, 2])
                drec = s3("drec", [P, 2])
                pdT = s3("pdT", [P, NB, KV, 4, 2])
                od = s3("od", [P, KT, NB])
                q_dec = s3("q_dec", [P, KT, NB, 2])
        fin = ExitStack()
        with fin:
            y_tok = sb("y_tok", [P, NBLK, D], F32, fin)
            y_dec = sb("y_dec", [NB, D], F32, fin)

        w_landed = [sem(f"w_landed{i}") for i in range(RAW)]
        hi_ready = sem("hi_ready")
        lo_ready = sem("lo_ready")
        w_used = sem("w_used")
        masks_in_s = sem("masks_landed")
        small_in = sem("small_landed")
        x_in = sem("x_landed")
        prep_pe = sem("prep_pe")
        prep_act = sem("prep_act")
        prep_dve = sem("prep_dve")
        consts_set = sem("consts_set")
        pads_set = sem("pads_set")
        ba_pe = sem("ba_pe")
        ba_act = sem("ba_act")
        ba_dve = sem("ba_dve")
        tables_done = sem("tables_done")
        norm_squared = sem("norm_squared")
        norm_added = sem("norm_added")
        norm_ln = sem("norm_ln")
        norm_rstd = sem("norm_rstd")
        norm_scaled = sem("norm_scaled")
        norm_hi = sem("norm_hi")
        norm_lo = sem("norm_lo")
        unit_squared = sem("unit_squared")
        part_half = sem("part_half")
        part_ready = sem("part_ready")
        pair_scaled = sem("pair_scaled")
        pair_hi = sem("pair_hi")
        pair_lo = sem("pair_lo")
        x_spilled = sem("x_spilled")
        x_back = sem("x_back")

        unit_copied = sem("unit_copied")
        conv_out = sem("conv_out")
        conv_step = sem("conv_step")
        pool_prev = sem("pool_prev")
        staged = sem("staged")
        silu_done = sem("silu_done")
        st_turned = sem("st_turned")
        st_copied = sem("st_copied")
        st_stored = sem("st_stored")
        sq_ready = sem("sq_ready")
        ss_ready = sem("ss_ready")
        rn_ln = sem("rn_ln")
        rn_ready = sem("rn_ready")
        qn_ready = sem("qn_ready")
        v_turned = sem("v_turned")
        v_copied = sem("v_copied")
        k_turned = sem("k_turned")
        k_copied = sem("k_copied")
        kmask_ready = sem("kmask_ready")
        gc_spread = sem("gc_spread")
        et_pre = sem("et_pre")
        et_exp = sem("et_exp")
        bst_ready = sem("bst_ready")
        kq_ready = sem("kq_ready")
        intra_ready = sem("intra_ready")
        nt_ready = sem("nt_ready")
        n_turned = sem("n_turned")
        n_copied = sem("n_copied")
        base_ready = sem("base_ready")
        pa_ready = sem("pa_ready")
        kk_ready = sem("kk_ready")
        inv_pe = sem("inv_pe")
        inv_act = sem("inv_act")
        inv_dve = sem("inv_dve")
        seq_pe = sem("seq_pe")
        seq_act = sem("seq_act")
        seq_dve = sem("seq_dve")
        qdec_ready = sem("qdec_ready")
        prompt_state_stored = sem("prompt_state_stored")
        dec_padded = sem("dec_padded")
        dec_pe = sem("dec_pe")
        dec_act = sem("dec_act")
        dec_dve = sem("dec_dve")
        s_loaded = sem("decode_state_landed")
        s_stored = sem("decode_state_stored")
        outer_pe = sem("outer_pe")
        outer_dve = sem("outer_dve")
        on_sq = sem("on_sq")
        on_ss = sem("on_ss")
        on_ln = sem("on_ln")
        on_rn = sem("on_rn")
        on_scaled = sem("on_scaled")
        on_gated = sem("on_gated")
        on_hi = sem("on_hi")
        head_done = sem("head_done")

        u_read = sem("u_read")
        f_silued = sem("f_silued")
        f_hi = sem("f_hi")
        f_lo = sem("f_lo")
        at_in = sem("at_in")
        at_brow = sem("at_brow")
        at_bst = sem("at_bst")
        at_pe = sem("at_pe")
        at_act = sem("at_act")
        bias_in = sem("bias_in")
        p_s = sem("p_s")
        p_add = sem("p_add")
        p_max = sem("p_max")
        p_exp = sem("p_exp")
        p_den = sem("p_den")
        p_norm = sem("p_norm")
        p_turn = sem("p_turn")
        p_copy = sem("p_copy")
        p_o = sem("p_o")
        p_ost = sem("p_ost")
        p_stage = sem("p_stage")
        p_hi = sem("p_hi")
        p_lo = sem("p_lo")
        d_pe = sem("d_pe")
        d_act = sem("d_act")
        d_dve = sem("d_dve")
        win_in = sem("win_in")
        q_zeroed = sem("q_zeroed")
        q_placed = sem("q_placed")
        y_stored = sem("y_stored")
        dk_turned = sem("dk_turned")
        dk_copied = sem("dk_copied")
        dk_scored = sem("dk_scored")
        y_turned = sem("y_turned")
        y_copied = sem("y_copied")
        stored = sem("stored")

        def after(eng, s, value):
            if not isinstance(value, int) or value > 0:
                eng.wait_ge(s, value)

        def bc(ap, dim, n):
            shape = list(ap.shape)
            return ap.unsqueeze(dim).broadcast_to(shape[:dim] + [n] + shape[dim:])

        def split_hi(act, c):
            q, s = c
            act.wait_ge(w_landed[s], 32 * q + 32)
            after(act, w_used, 4 * q + (s - SPL + 1))
            nc.scalar.activation(w_hi[:, s % SPL, :], w_raw[:, s, :], ACT.Copy).then_inc(hi_ready, 1)

        def split_lo(eng, c):
            q, s = c
            ops = nc.gpsimd if eng is nc.gpsimd else nc.vector
            eng.wait_ge(hi_ready, 4 * q + (s + 1))
            after(eng, w_used, 4 * q + (s - SPL + 1))
            ops.tensor_tensor(w_lo[:, s % SPL, :], w_raw[:, s, :], w_hi[:, s % SPL, :].bitcast(F32),
                                    ALU.subtract).then_inc(lo_ready, 1)

        def tiles(pe, c, tl, part=None):
            q, s = c
            if part in (None, 0):
                pe.wait_ge(lo_ready, 4 * q + (s + 1))
            for n, (t, bk, xh, xl, first, last) in enumerate(tl):
                wh = w_hi[:, s % SPL, t * P:(t + 1) * P]
                wl = w_lo[:, s % SPL, t * P:(t + 1) * P]
                nc.tensor.matmul(bank[bk][:, 0:T], wh, xh, start=first, stop=False)
                nc.tensor.matmul(bank[bk][:, 0:T], wh, xl, start=False, stop=False)
                m = nc.tensor.matmul(bank[bk][:, 0:T], wl, xh, start=False, stop=last)
            if part in (None, 1):
                m.then_inc(w_used, 1)
            return m

        def load(sp, c, *halves):
            q, s = c
            after(sp, lo_ready, 4 * q + (s - RAW + 1))
            sp.wait_ge(masks_in_s, 16)
            for i, src in enumerate(halves):
                dst = w_raw[:, s, i * ELEMS // 2:(i + 1) * ELEMS // 2]
                sp.dma_start(dst.rearrange("p (k n) -> p k n", k=src.shape[1]), src).then_inc(w_landed[s], 16)

        def rows2(view, k, n, cols):
            return view[:, k:k + n // 2, cols], view[:, k + n // 2:k + n, cols]

        w_in_v = w_in[0].rearrange("(k p) n -> p k n", p=P)
        w_out_v = w_out[0].rearrange("(k p) n -> p k n", p=P)
        w_gu_v = [w_gate_up[l].rearrange("(k p) n -> p k n", p=P) for l in range(2)]
        w_down_v = [w_down[l].rearrange("(k p) n -> p k n", p=P) for l in range(2)]
        w_kv_v = w_kv.rearrange("(k p) n -> p k n", p=P)
        w_q_v = w_q[0].rearrange("(k p) n -> p k n", p=P)
        w_o_v = w_o[0].rearrange("(k p) n -> p k n", p=P)

        U_OUT = 2
        U_GU = [U_OUT + 4, 0]
        U_DOWN = [U_GU[0] + FT // 2, 0]
        U_KV = U_DOWN[0] + 4
        U_Q = U_KV + 1
        U_O = U_Q + 4
        U_GU[1] = U_O + 4
        U_DOWN[1] = U_GU[1] + FT // 2
        U_END = U_DOWN[1] + 4

        NORMS = {"ffn0": (0, 2, 0, U_GU[0], C_OUT), "kv": (1, 4, 1, U_KV, C_DOWN[0]), "mix1": (2, 1, None, 0, 0),
                 "ffn1": (3, 3, 2, U_GU[1], C_O), "final": (4, 5, 3, U_END, 0)}
        PAIRS = KT // 2
        UNITS_SQUARED = [U_OUT, U_DOWN[0], U_O, U_DOWN[1]]
        YPARTS = 4
        TURNS = 6 + KT

        def first_norm_act(act):
            act.wait_ge(prep_act, TURNS)
            for t in range(KT):
                if t >= 2:
                    act.wait_ge(norm_added, t - 1)
                nc.scalar.activation(norm_sq[:, t % 2, :], x_first[:, t, :], ACT.Square).then_inc(norm_squared, 1)
            act.wait_ge(norm_added, KT)
            root_act(act, 0)
            for j in range(KT // 2):
                act.wait_ge(norm_scaled, j + 1)
                nc.scalar.activation(h_hi[:, 2 * j:2 * j + 2, :], (norm_h, norm_sq)[j % 2][:, :, :], ACT.Copy
                                     ).then_inc(norm_hi, 1)

        def root_act(act, k):
            nc.scalar.preload_act_table_set("natural_log_exp_and_others")
            nc.scalar.activation(rstd[:, :], bank[0][:, 0:T], ACT.Ln, bias=bias_c[:, 0:1],
                                 scale=1.0 / D).then_inc(norm_ln, 1)
            act.wait_ge(norm_ln, k + 1)
            nc.scalar.activation(rstd[:, :], rstd[:, :], ACT.Exp, scale=-0.5).then_inc(norm_rstd, 1)

        def first_norm_pe(pe):
            for t in range(KT):
                pe.wait_ge(norm_squared, t + 1)
                nc.tensor.matmul(bank[0][:, 0:T], ones, norm_sq[:, t % 2, :], start=(t == 0),
                                 stop=(t == KT - 1)).then_inc(norm_added, 1)

        def first_norm_dve(dve):
            dve.wait_ge(norm_rstd, 1)
            for j in range(KT // 2 + 1):
                if j < KT // 2:
                    if j >= 2:
                        dve.wait_ge(norm_lo, j - 1)
                    for t in (2 * j, 2 * j + 1):
                        m = nc.vector.scalar_tensor_tensor((norm_h, norm_sq)[j % 2][:, t % 2, :], x_first[:, t, :],
                                                           gains[:, t:t + 1], rstd[:, :], ALU.mult, ALU.mult)
                    m.then_inc(norm_scaled, 1)
                if j:
                    dve.wait_ge(norm_hi, j)
                    nc.vector.tensor_tensor(h_lo[:, 2 * j - 2:2 * j, :], (norm_h, norm_sq)[(j - 1) % 2][:, :, :],
                                            h_hi[:, 2 * j - 2:2 * j, :].bitcast(F32), ALU.subtract).then_inc(norm_lo, 1)

        def square_unit(act, k, n):
            act.wait_ge(u_read, n + (UNITS_SQUARED[k] + 1))
            after(act, part_ready, n + 4 * k)
            nc.scalar.activation(f_sq[:, :, :], x_res[:, ds(4 * n, 4), :], ACT.Square).then_inc(unit_squared, 1)

        def part_unit(dve, k, n):
            dve.wait_ge(unit_squared, n + (4 * k + 1))
            nc.vector.tensor_tensor(f_sq[:, 0:2, :], f_sq[:, 0:2, :], f_sq[:, 2:4, :], ALU.add).then_inc(part_half, 1)
            dve.wait_ge(part_half, n + (4 * k + 1))
            nc.vector.tensor_tensor(part[:, ds(n, 1), :], f_sq[:, 0:1, :], f_sq[:, 1:2, :], ALU.add
                                    ).then_inc(part_ready, 1)

        def norm_pe(pe, which):
            k, units = NORMS[which][2:4]
            pe.wait_ge(u_read, units - 1)
            for u in range(4):
                pe.wait_ge(part_ready, 4 * k + u + 1)
                m = nc.tensor.matmul(bank[0][:, 0:T], ones, part[:, u, :], start=(u == 0), stop=(u == 3))
            m.then_inc(norm_added, 1)

        def norm_act(act, which):
            k = NORMS[which][2]
            if k is not None:
                act.wait_ge(norm_added, KT + k + 1)
                root_act(act, k + 1)
            if which != "final":
                hi_pair(act, which, 0)

        def norm_dve(dve, which):
            k = NORMS[which][2]
            if k is not None:
                dve.wait_ge(norm_rstd, k + 2)
            if which != "final":
                scale_pair(dve, which, 0)

        def normed(which):
            return (ao_hi, ao_lo) if which == "mix1" else (h_hi, h_lo)

        def scale_pair(dve, which, j):
            n, g = NORMS[which][0:2]
            after(dve, pair_lo, PAIRS * n + j)
            for t in (2 * j, 2 * j + 1):
                m = nc.vector.scalar_tensor_tensor(norm_h[:, t % 2, :], x_res[:, t, :],
                                                   gains[:, g * KT + t:g * KT + t + 1], rstd[:, :], ALU.mult, ALU.mult)
            m.then_inc(pair_scaled, 1)

        def hi_pair(act, which, j):
            n, _, _, _, chunks = NORMS[which]
            if j == 0 and chunks:
                act.wait_ge(w_used, chunks)
            act.wait_ge(pair_scaled, PAIRS * n + j + 1)
            nc.scalar.activation(normed(which)[0][:, 2 * j:2 * j + 2, :], norm_h[:, :, :], ACT.Copy
                                 ).then_inc(pair_hi, 1)

        def lo_pair(dve, which, j):
            n = NORMS[which][0]
            hi, lo = normed(which)
            dve.wait_ge(pair_hi, PAIRS * n + j + 1)
            nc.vector.tensor_tensor(lo[:, 2 * j:2 * j + 2, :], norm_h[:, :, :],
                                    hi[:, 2 * j:2 * j + 2, :].bitcast(F32), ALU.subtract).then_inc(pair_lo, 1)

        def pool_after_delta(pool):
            pool.wait_ge(head_done, GROUPS)
            pool.wait_ge(s_stored, 32 * GROUPS)
            pool.wait_ge(prompt_state_stored, 16 * GROUPS)
            pool.wait_ge(st_stored, 96 * GROUPS)
            pool.dma_start(x_res[:, :, :].rearrange("p t n -> p (t n)"), x_spill).then_inc(x_back, 16)

            def first_splits(base, n):
                pool.wait_ge(lo_ready, base + 1)
                for j in range(n):
                    split_lo(pool, chunk(base, RAW, 0, j + 1))

            first_splits(C_GU[0], PAIRS)
            first_splits(C_KV, UNIT["kv"] + PAIRS)
            pool.wait_ge(w_used, C_KV)
            pool.dma_start(sink_all[:, :], sinks.broadcast_to([P, HEADS])).then_inc(at_in, 16)
            for dst, cache in ((k_win, cache_k), (v_win, cache_v)):
                pool.dma_start(dst[0:WINDOW - 1, :, :, :], cache[:, 1:WINDOW].rearrange("b w k d -> w b k d")
                               ).then_inc(win_in, 16)
            for i in range(4):
                pool.dma_start(bias_d[HEADS * i:HEADS * (i + 1), :], bias_rows[:, WINDOW:2 * WINDOW]).then_inc(bias_in, 16)
                pool.dma_start(sink_d[HEADS * i:HEADS * (i + 1), :], sinks.rearrange("a h -> h a")).then_inc(bias_in, 16)
            pool.memset(q_dec[:, :, :, :], 0.0).then_inc(q_zeroed, 1)
            pool.wait_ge(d_act, 1)
            for o_, dst in enumerate((k_win, v_win)):
                pool.dma_start(dst[WINDOW - 1:WINDOW, :, :, :], newtok[:, o_, :].rearrange("b (k d) -> b k d", k=KV)
                               ).then_inc(win_in, 16)
            for o_, dst in enumerate((kwin_s, vwin_s)):
                pool.dma_start(dst[:, WINDOW - 1, :, :].rearrange("b k d -> b (k d)"), newtok[:, o_, :]
                               ).then_inc(stored, 16)
            pool.wait_ge(d_act, 3)
            pool.dma_start(kwin_p[0].rearrange("w k d -> w (k d)"), ktw[:, :]).then_inc(stored, 16)
            pool.dma_start(vwin_p[0], vtk[:, 1, :, :]).then_inc(stored, 16)
            pool.wait_ge(d_dve, 10)
            pool.wait_ge(d_pe, 6)

            def stage(kv):
                later = not isinstance(kv, int) or kv
                if later:
                    pool.wait_ge(p_s, 4 * kv)
                pool.tensor_copy(k_st[:, :], kdup[:, ds(kv, 1), :]).then_inc(p_stage, 1)
                pool.tensor_copy(q_st[:, :, :], qT[:, ds(4 * kv, 4), 0:NP]).then_inc(p_stage, 1)
                if later:
                    pool.wait_ge(p_max, 20 * kv)
                rows = bias_tiles[8 * kv:8 * kv + 8, :, :]
                src = bass.AP(rows.tensor, rows.offset + WINDOW - 1,
                              [[3 * WINDOW - 1, P], [P * 3 * WINDOW, 8], [1, 2 * WINDOW]])
                pool.dma_start(bias[:, :, :], src).then_inc(bias_in, 16)
                pool.tensor_copy(sink_st[:, :], sink_all[:, ds(8 * kv, 8)]).then_inc(p_stage, 1)
                if later:
                    pool.wait_ge(p_o, 4 * kv)
                pool.tensor_copy(v_st[:, :, :], vtk[:, :, ds(kv, 1), :]).then_inc(p_stage, 1)

            pool.wait_ge(at_in, 48)
            pool.wait_ge(at_bst, 32)
            for kv in range(KV):
                stage(kv)
            first_splits(C_GU[1], PAIRS)

        def act_after_delta(act):
            def columns(base, per, k, last=False, done=0):
                def once(i, final=False, done=0):
                    for j in range(done, 2 * per):
                        if not (final and j == 2 * per - 1):
                            split_hi(act, chunk(base, 2 * per, i, j + 1))
                        if j in (per, 2 * per - 1):
                            square_unit(act, k, 2 * i + j // (per + 1))
                if last or done:
                    once(0, done=done)
                    once(1, last)
                else:
                    with act.Fori(0, 2) as i:
                        once(i)

            def ffn(l):
                per = UNIT["gu"]

                def silu(n, u):
                    act.wait_ge(w_used, per * n + (C_GU[l] + per))
                    act.wait_ge(u_read, n + U_GU[l])
                    for t in range(2):
                        m = nc.scalar.activation(f_silu[:, t, :], bank[4 * u + t][:, 0:T], ACT.Silu)
                    m.then_inc(f_silued, 1)

                def hidden_hi(n):
                    act.wait_ge(u_read, n + (U_GU[l] + 1))
                    nc.scalar.activation(a_hi[:, ds(2 * n, 2), :], f_h[:, :, :], ACT.Copy).then_inc(f_hi, 1)

                def once(i, first=False):
                    for j in range(2 * per):
                        split_hi(act, chunk(C_GU[l], 2 * per, i, j + 1))
                        if first and j + 1 < PAIRS:
                            hi_pair(act, f"ffn{l}", j + 1)
                        if j == 0 and not first:
                            silu(2 * i - 1, 1)
                        elif j == 1 and not first:
                            hidden_hi(2 * i - 1)
                        elif j == per:
                            silu(2 * i, 0)
                        elif j == per + 1:
                            hidden_hi(2 * i)
                once(0, True)
                with act.Fori(1, FT // 4) as i:
                    once(i)
                silu(FT // 2 - 1, 1)
                hidden_hi(FT // 2 - 1)
                columns(C_DOWN[l], UNIT["down"], 2 * l + 1, last=l == 1)

            columns(C_OUT, UNIT["out"], 0, done=12)
            norm_act(act, "ffn0")
            ffn(0)
            norm_act(act, "kv")
            for j in range(UNIT["kv"]):
                split_hi(act, chunk(C_KV, RAW, 0, j + 1))
                hi_pair(act, *(("kv", j + 1) if j + 1 < PAIRS else ("mix1", 0)))

            def queries(i):
                per = UNIT["q"]
                for j in range(2 * per):
                    split_hi(act, chunk(C_Q, 2 * per, i, j + 1))
                    if i == 0 and j + 1 < PAIRS:
                        hi_pair(act, "mix1", j + 1)
                    if i == 0 and j == 1:
                        act.wait_ge(w_used, C_Q)
                        for n in range(4):
                            nc.scalar.activation(kvT[:, n, :], bank[n][:, 0:T], ACT.Copy).then_inc(at_act, 1)
                    if i == 0 and 2 <= j < 4:
                        for kv in (2 * (j - 2), 2 * (j - 2) + 1):
                            half = HD * (kv % 2)
                            for to in (0, HD):
                                m = nc.scalar.activation(kdup[to:to + HD, kv, :], bank[kv // 2][half:half + HD, 0:NP],
                                                         ACT.Copy)
                        if j == 3:
                            m.then_inc(u_read, 1)
                    if j % per == per - 1:
                        u = j // per
                        act.wait_ge(w_used, 2 * per * i + (C_Q + per * (u + 1)))
                        for n in range(4):
                            m = nc.scalar.activation(qT[:, 8 * i + 4 * u + n, :], bank[4 * (1 - u) + n][:, 0:T], ACT.Copy)
                        m.then_inc(u_read, 1)

            queries(0)
            queries(1)

            act.wait_ge(d_pe, 3)
            nc.scalar.activation(newtok[:, :, :], bank[1][0:NB, :].rearrange("p (j n) -> p j n", j=2),
                                 ACT.Copy).then_inc(d_act, 1)
            nc.scalar.activation(ktw[:, :], bank[2][:, 0:2 * P], ACT.Copy).then_inc(d_act, 1)
            nc.scalar.activation(vtk[:, 1, :, :], bank[2][:, 2 * P:4 * P].rearrange("p (k d) -> p k d", k=KV),
                                 ACT.Copy).then_inc(d_act, 1)
            nc.scalar.activation(vtk[:, 0, :, :], bank[3][:, 0:2 * P].rearrange("p (k d) -> p k d", k=KV),
                                 ACT.Copy).then_inc(d_act, 1)
            act.wait_ge(q_zeroed, 1)
            for half in range(2):
                r = slice(HD * half, HD * (half + 1))
                nc.scalar.activation(q_dec[r, :, :, half], qT[r, :, NP:T], ACT.Copy).then_inc(q_placed, 1)
            for b in range(NB):
                act.wait_ge(dk_turned, b + 1)
                if b >= 2:
                    act.wait_ge(dk_scored, b - 1)
                src = bank[4 + b % 2][:, 0:2 * P].rearrange("p (j n) -> p j n", j=2)
                for e in range(2):
                    for to in (0, HD):
                        m = nc.scalar.activation(k_t[to:to + HD, b % 2, e::2, :], src[HD * e:HD * (e + 1), :, :],
                                                 ACT.Copy)
                m.then_inc(dk_copied, 1)
            act.wait_ge(dk_scored, NB)
            nc.scalar.activation(sT[:, :, :], bank[6][:, 0:2 * P], ACT.Copy, scale=ATT).then_inc(d_act, 2)
            act.wait_ge(d_dve, 5)
            for t in range(2):
                nc.scalar.activation(sdc[:, t, :], sdc[:, t, :], ACT.Exp, bias=dnm[:, t:t + 1],
                                     accum_out=dsum[:, t:t + 1]).then_inc(d_act, 1)
            act.wait_ge(d_dve, 6)
            nc.scalar.activation(des[:, :], des[:, :], ACT.Exp).then_inc(d_act, 1)
            act.wait_ge(d_pe, 5)
            nc.scalar.activation(pdT[:, :, :, :, :], bank[1][:, 0:NB * HEADS], ACT.Copy).then_inc(d_act, 1)
            act.wait_ge(d_pe, 6)
            nc.scalar.activation(od[:, :, :], bank[2][:, 0:KT * NB], ACT.Copy).then_inc(d_act, 1)
            act.wait_ge(d_act, 11)
            nc.scalar.activation(ao_hi[:, :, NP:T], od[:, :, :], ACT.Copy).then_inc(d_act, 1)

            def exponentials(kv, p):
                n = 4 * kv + p
                b = p % 2
                act.wait_ge(p_max, 5 * n + 4)
                for i in range(4):
                    s = scores_sb[:, b, i % 2, 0:256] if i < 2 else scores_sb[:, b, i % 2, 256:384]
                    nc.scalar.activation(s, s, ACT.Exp, bias=snm[:, b, i:i + 1],
                                         accum_out=ssum[:, b, i:i + 1]).then_inc(p_exp, 1)
                act.wait_ge(p_max, 5 * n + 5)
                nc.scalar.activation(ses[:, b, :], ses[:, b, :], ACT.Exp).then_inc(p_exp, 1)

            def attend(kv):
                exponentials(kv, 0)
                for p in range(4):
                    n = 4 * kv + p
                    if p < 3:
                        exponentials(kv, p + 1)
                    act.wait_ge(p_turn, n + 1)
                    if p or not isinstance(kv, int) or kv:
                        act.wait_ge(p_o, n)
                    nc.scalar.activation(pT[:, 0:4, :], bank[4][:, :], ACT.Copy).then_inc(p_copy, 1)
                    nc.scalar.activation(pT[:, 4:6, :], bank[5][:, 0:2 * P], ACT.Copy).then_inc(p_copy, 1)
                    act.wait_ge(p_o, n + 1)
                    if p == 0 and (not isinstance(kv, int) or kv):
                        act.wait_ge(p_lo, kv)
                    nc.scalar.activation(o_st[:, p, :], bank[6][:, 0:NP], ACT.Copy).then_inc(p_ost, 1)
                act.wait_ge(p_ost, 4 * kv + 4)
                nc.scalar.activation(ao_hi[:, ds(4 * kv, 4), 0:NP], o_st[:, :, :], ACT.Copy).then_inc(p_hi, 1)

            attend(0)
            with act.Fori(1, KV) as kv:
                attend(kv)
            columns(C_O, UNIT["o"], 2)
            norm_act(act, "ffn1")
            ffn(1)
            norm_act(act, "final")
            for t in range(KT):
                act.wait_ge(y_turned, t + 1)
                bk = bank[2 + t % 4]
                nc.scalar.activation(y_tok[:, :, t * P:(t + 1) * P], bk[:, 0:NP].rearrange("p (b n) -> p b n", b=NBLK),
                                     ACT.Copy).then_inc(y_copied, 1)
                nc.scalar.activation(y_dec[:, t * P:(t + 1) * P], bk[0:NB, NP:NP + P], ACT.Copy).then_inc(y_copied, 1)
            act.wait_ge(y_copied, 2 * KT)
            act.dma_start(y_sample.rearrange("b t n -> (b t) n"), y_dec[:, :]).then_inc(y_stored, 16)
            act.wait_ge(y_stored, 16 * (YPARTS + 1))
            act.wait_ge(stored, 16 * 7)

        def pe_after_delta(pe):
            def columns(base, per, U0, xh, xl, flip=0, which=None, at_end=None, done=0):
                def once(i, done=0):
                    for j in range(done, 2 * per):
                        u, k = j // per, 2 * (j % per)
                        if j % per == 0:
                            pe.wait_ge(u_read, 2 * i + (U0 + u - 1))
                        if which and i == 0 and j < PAIRS:
                            pe.wait_ge(pair_lo, PAIRS * NORMS[which][0] + j + 1)
                        if at_end and j == per - 1:
                            pe.wait_ge(*at_end)
                        b = 4 * ((u + flip) % 2)
                        tiles(pe, chunk(base, 2 * per, i, j),
                              [(4 * kk + n, b + n, xh[:, k + kk, :], xl[:, k + kk, :], k + kk == 0,
                                k + kk == 2 * per - 1) for kk in range(2) for n in range(4)])
                if which or done:
                    once(0, done)
                    once(1)
                else:
                    with pe.Fori(0, 2) as i:
                        once(i)

            def ffn(l):
                def once(i, first=False):
                    for j in range(2 * UNIT["gu"]):
                        u, k = j // UNIT["gu"], 2 * (j % UNIT["gu"])
                        if k == 0:
                            pe.wait_ge(u_read, 2 * i + (U_GU[l] + u - 1))
                        if first and j < PAIRS:
                            pe.wait_ge(pair_lo, PAIRS * NORMS[f"ffn{l}"][0] + j + 1)
                        tiles(pe, chunk(C_GU[l], 2 * UNIT["gu"], i, j),
                              [(4 * (n // 2) + 2 * kk + n % 2, 4 * u + n, h_hi[:, k + kk, :], h_lo[:, k + kk, :], k + kk == 0,
                                k + kk == KT - 1) for kk in range(2) for n in range(4)])
                once(0, True)
                with pe.Fori(1, FT // 4) as i:
                    once(i)
                pe.wait_ge(f_lo, FT // 2 * (l + 1) - 1)
                columns(C_DOWN[l], UNIT["down"], U_DOWN[l], a_hi, a_lo, at_end=(f_lo, FT // 2 * (l + 1)))

            columns(C_OUT, UNIT["out"], U_OUT, o_hi, o_lo, at_end=(head_done, GROUPS), done=12)
            norm_pe(pe, "ffn0")
            ffn(0)
            norm_pe(pe, "kv")
            for j in range(UNIT["kv"]):
                pe.wait_ge(pair_lo, PAIRS * NORMS["kv"][0] + j + 1)
                tiles(pe, chunk(C_KV, RAW, 0, j),
                      [(4 * kk + n, n, h_hi[:, 2 * j + kk, :], h_lo[:, 2 * j + kk, :], 2 * j + kk == 0,
                        2 * j + kk == KT - 1) for kk in range(2) for n in range(4)])
            columns(C_Q, UNIT["q"], U_Q, ao_hi, ao_lo, flip=1, which="mix1")
            pe.wait_ge(u_read, U_O)
            for j in range(4):
                m = nc.tensor.transpose(bank[1][0:NB, j * P:(j + 1) * P], kvT[:, j, NP:T], ident)
            m.then_inc(d_pe, 1)
            for j in range(4):
                m = nc.tensor.transpose(bank[2][:, j * P:(j + 1) * P], kvT[:, j, P:2 * P], ident)
            m.then_inc(d_pe, 1)
            for j in range(2):
                m = nc.tensor.transpose(bank[3][:, j * P:(j + 1) * P], kvT[:, 2 + j, 0:P], ident)
            m.then_inc(d_pe, 1)
            pe.wait_ge(win_in, 64)
            pe.wait_ge(q_placed, 2)
            for b in range(NB + 1):
                if b < NB:
                    if b >= 2:
                        pe.wait_ge(dk_copied, b - 1)
                    for j in range(2):
                        m = nc.tensor.transpose(bank[4 + b % 2][:, j * P:(j + 1) * P],
                                                k_win[:, b, 2 * j:2 * j + 2, :], ident)
                    m.then_inc(dk_turned, 1)
                if b:
                    r = b - 1
                    pe.wait_ge(dk_copied, b)
                    for kv in range(KV):
                        at = 32 * r + 8 * kv
                        m = nc.tensor.matmul(bank[6][:, at:at + 8], k_t[:, r % 2, kv, :],
                                             q_dec[:, 4 * kv:4 * kv + 4, r, :], start=True, stop=True)
                    m.then_inc(dk_scored, 1)
            pe.wait_ge(d_act, 6)
            for t in range(2):
                m = nc.tensor.transpose(bank[0][:, t * P:(t + 1) * P], sT[:, 64 * t:64 * (t + 1), :], ident)
            m.then_inc(d_pe, 1)
            pe.wait_ge(d_dve, 9)
            for t in range(2):
                m = nc.tensor.transpose(bank[1][:, t * P:(t + 1) * P], sdc[:, t, :], ident)
            m.then_inc(d_pe, 1)
            pe.wait_ge(d_act, 10)
            for b in range(NB):
                for kv in range(KV):
                    for half in range(2):
                        lo_ = HD * half
                        out = bank[2][:, 0:KT * NB].rearrange("p (t b) -> p t b", b=NB)
                        m = nc.tensor.matmul(out[lo_:lo_ + HD, 4 * kv:4 * kv + 4, b], v_win[:, b, kv, :],
                                             pdT[:, b, kv, :, half], start=True, stop=True)
            m.then_inc(d_pe, 1)

            def scores(kv, p):
                n = 4 * kv + p
                if p >= 2 or not isinstance(kv, int) or kv:
                    pe.wait_ge(p_add, 4 * (n - 1))
                if p == 0:
                    pe.wait_ge(p_stage, 4 * kv + 3)
                for h in range(2):
                    r = slice(HD * h, HD * (h + 1))
                    s = bank[2 * (p % 2) + h]
                    nc.tensor.matmul(s[:, 0:2 * P], q_st[r, p, P:2 * P], k_st[r, :], start=True, stop=True)
                    m = nc.tensor.matmul(s[:, 2 * P:3 * P], q_st[r, p, 0:P], k_st[r, 0:P], start=True, stop=True)
                m.then_inc(p_s, 1)

            def attend(kv):
                scores(kv, 0)
                scores(kv, 1)
                for p in range(4):
                    n = 4 * kv + p
                    b = p % 2
                    pe.wait_ge(p_norm, 2 * n + 2)
                    if p or not isinstance(kv, int) or kv:
                        pe.wait_ge(p_copy, 2 * n)
                    for h in range(2):
                        for kb in range(2):
                            nc.tensor.transpose(bank[4][:, (2 * h + kb) * P:(2 * h + kb + 1) * P],
                                                scores_sb[:, b, h, kb * P:(kb + 1) * P], ident)
                        m = nc.tensor.transpose(bank[5][:, h * P:(h + 1) * P], scores_sb[:, b, h, 2 * P:3 * P], ident)
                    m.then_inc(p_turn, 1)
                    if p < 2:
                        scores(kv, p + 2)
                    pe.wait_ge(p_copy, 2 * n + 2)
                    if p == 0:
                        pe.wait_ge(p_stage, 4 * kv + 4)
                    if p or not isinstance(kv, int) or kv:
                        pe.wait_ge(p_ost, n)
                    for h in range(2):
                        r = slice(HD * h, HD * (h + 1))
                        for kb in range(2):
                            nc.tensor.matmul(bank[6][r, P:2 * P], v_st[:, kb, :], pT[:, 2 * h + kb, :],
                                             start=(kb == 0), stop=(kb == 1))
                        m = nc.tensor.matmul(bank[6][r, 0:P], v_st[:, 0, :], pT[:, 4 + h, :], start=True, stop=True)
                    m.then_inc(p_o, 1)

            attend(0)
            with pe.Fori(1, KV) as kv:
                attend(kv)
            pe.wait_ge(p_lo, KV)
            pe.wait_ge(d_dve, 10)
            columns(C_O, UNIT["o"], U_O, ao_hi, ao_lo)
            norm_pe(pe, "ffn1")
            ffn(1)
            norm_pe(pe, "final")
            for t in range(KT):
                pe.wait_ge(norm_scaled, KT // 2 + t + 1)
                after(pe, y_copied, 2 * (t - 3))
                bk = bank[2 + t % 4]
                for b in range(NBLK):
                    nc.tensor.transpose(bk[:, b * P:(b + 1) * P], norm_h[:, t % 2, b * P:(b + 1) * P], ident)
                nc.tensor.transpose(bk[0:NB, NP:NP + P], norm_h[:, t % 2, NP:T], ident).then_inc(y_turned, 1)

        block = ctx.enter_context(nc.Block())

        w_in_n = w_in.shape[2]
        delta_s_v = delta_s[0].rearrange("b h k v -> k h b v")
        state_v = state_delta[0].rearrange("b h k v -> k h b v")
        delta_p_v = delta_p[0, 0].rearrange("h k v -> k h v")

        def state_out(eng, G):
            eng.wait_ge(outer_dve, 16 * G + 16)
            eng.wait_ge(masks_in_s, 16)
            for h in range(2):
                eng.dma_start(delta_s_v[:, ds(2 * G + h, 1), :, :], s_dec[:, h:h + 1, :, :]).then_inc(s_stored, 16)
            eng.wait_ge(seq_dve, 7 * G + 7)
            eng.wait_ge(masks_in_s, 16)
            eng.dma_start(delta_p_v[:, ds(2 * G, 2), :], S2[:, :, :]).then_inc(prompt_state_stored, 16)

        def conv_rows_out(eng, G):
            eng.wait_ge(st_copied, G + 1)
            eng.wait_ge(masks_in_s, 16)
            for t, col in ((0, G * P), (1, G * P + D), (2, G * 2 * P + 2 * D)):
                n = 1 if t < 2 else 2
                eng.dma_start(conv_p[0, 0, :, ds(col, n * P)], strow[0:3, t:t + n, :]).then_inc(st_stored, 16)
                eng.dma_start(conv_s[0, :, 2, ds(col, n * P)], strow[3:3 + NB, t:t + n, :]).then_inc(st_stored, 16)

        def state_back(eng, G):
            after(eng, s_stored, 32 * G)
            eng.wait_ge(masks_in_s, 16)
            for h in range(2):
                eng.dma_start(s_dec[:, h:h + 1, :, :], state_v[:, ds(2 * G + h, 1), :, :]).then_inc(s_loaded, 16)

        @block.sync
        def _(sp):
            sp.dma_start(masks[:, :], masks_in).then_inc(masks_in_s, 16)
            for r, ap in enumerate((norm_mix[0], norm_mix[1], norm_ffn[0], norm_ffn[1], norm_kv, norm_final)):
                sp.dma_start(rows_in[r * KT:(r + 1) * KT, 0, :],
                             ap.rearrange("(t c) -> t c", c=P)).then_inc(small_in, 16)
            sp.dma_start(rows_in[6 * KT:6 * KT + 1, 0, :], gnorm).then_inc(small_in, 16)
            for j in range(4):
                sp.dma_start(rows_in[CT * (j % 2):CT * (j % 2 + 1), 1 + j // 2, :],
                             conv_w[0, j].rearrange("(t c) -> t c", c=P)).then_inc(small_in, 16)
            sp.dma_start(sc_rows[:, :], state_conv[0].rearrange("b j n -> (b j) n")).then_inc(small_in, 16)
            sp.dma_start(x_rows[:, :, :], x_prompt[0].rearrange("(b p) n -> p b n", p=P)).then_inc(x_in, 16)
            sp.dma_start(x_rows_d[:, :], x_sample.rearrange("b t n -> (b t) n")).then_inc(x_in, 16)
            sp.dma_start(hcol[:, 0:1], a_log.rearrange("a h -> h a")).then_inc(small_in, 16)
            sp.dma_start(hcol[:, 1:2], dt_bias.rearrange("a h -> h a")).then_inc(small_in, 16)

            for j in range(2):
                load(sp, chunk(C_BA, RAW, 0, j), *rows2(w_in_v, 8 * j, 8, slice(w_in_n - P, w_in_n)))

            def group_weights(g, first=False, second=False):
                for j in range(12):
                    c, u, k = chunk(C_IN, 12, g, j), j // 4, 4 * (j % 4)
                    if u == 0:
                        load(sp, c, w_in_v[:, k:k + 4, ds(g * P, P)], w_in_v[:, k:k + 4, ds(g * P + D, P)])
                    else:
                        load(sp, c, *rows2(w_in_v, k, 4, ds(g * 2 * P + 2 * D * u, 2 * P)))
                    if j == 4 and not first and not second:
                        state_out(sp, g - 2)
                    if j == 6 and not first:
                        conv_rows_out(sp, g - 1)
                    if j == 8 and not first:
                        state_back(sp, g - 1)

            group_weights(0, first=True)
            group_weights(1, second=True)
            with sp.Fori(2, GROUPS) as g:
                group_weights(g)

            def columns(base, per, view):
                with sp.Fori(0, 2) as i:
                    for j in range(2 * per):
                        u, k = j // per, 2 * (j % per)
                        load(sp, chunk(base, 2 * per, i, j), *rows2(view, k, 2, ds(i * 1024 + u * 512, 512)))

            def ffn_weights(l):
                with sp.Fori(0, FT // 4) as i:
                    for j in range(2 * UNIT["gu"]):
                        u, k = j // UNIT["gu"], 2 * (j % UNIT["gu"])
                        load(sp, chunk(C_GU[l], 2 * UNIT["gu"], i, j),
                             w_gu_v[l][:, k:k + 2, ds(i * 512 + u * 256, 256)],
                             w_gu_v[l][:, k:k + 2, ds(i * 512 + (u * 256 + FF), 256)])
                columns(C_DOWN[l], UNIT["down"], w_down_v[l])

            columns(C_OUT, UNIT["out"], w_out_v)
            ffn_weights(0)
            for j in range(UNIT["kv"]):
                load(sp, chunk(C_KV, RAW, 0, j), *rows2(w_kv_v, 2 * j, 2, slice(0, 512)))
            columns(C_Q, UNIT["q"], w_q_v)
            columns(C_O, UNIT["o"], w_o_v)
            ffn_weights(1)
            for i in range(YPARTS):
                n = D // YPARTS
                sp.wait_ge(y_copied, 2 * KT // YPARTS * (i + 1))
                sp.dma_start(y_prompt[0].rearrange("(b p) n -> p b n", p=P)[:, :, n * i:n * (i + 1)],
                             y_tok[:, :, n * i:n * (i + 1)]).then_inc(y_stored, 16)

        @block.gpsimd
        def _(pool):
            pool.memset(bias_c[:, 0:1], EPS).then_inc(consts_set, 1)
            pool.memset(bias_c[:, 1:2], float(np.log(QS))).then_inc(consts_set, 1)
            pool.memset(gb_pad[:, :, :], 0.0).then_inc(consts_set, 1)
            pool.dma_start(buckets[:, :], buckets_in).then_inc(at_in, 16)
            pool.dma_start(relb[:, :], rel_bias).then_inc(at_in, 16)
            pool.wait_ge(prep_act, TURNS)
            pool.dma_start(x_spill, x_first[:, :, :].rearrange("p t n -> p (t n)")).then_inc(x_spilled, 16)
            pool.wait_ge(at_brow, 1)
            pool.dma_start(bias_rows, brow[:, :]).then_inc(at_bst, 16)
            pool.dma_start(conv_s[0, :, 0:2, :], state_conv[0, :, 1:3, :]).then_inc(stored, 16)
            pool.dma_start(kwin_s[:, 0:WINDOW - 1], cache_k[:, 1:WINDOW]).then_inc(stored, 16)
            pool.dma_start(vwin_s[:, 0:WINDOW - 1], cache_v[:, 1:WINDOW]).then_inc(stored, 16)
            pool.wait_ge(x_spilled, 16)
            pool.wait_ge(at_bst, 16)
            pool.dma_start(bias_tiles, bias_rows.unsqueeze(1).broadcast_to([HEADS, P, 3 * WINDOW])).then_inc(at_bst, 16)
            pool.wait_ge(norm_lo, KT // 2)
            pool.wait_ge(tables_done, 2)
            pool.memset(craw[:, :, 0:3], 0.0).then_inc(pads_set, 1)
            for t in (kq_diag[:, :], kv_pad[:, :, :], dec_qk[:, :]):
                pool.memset(t, 0.0).then_inc(pads_set, 1)

            def cached_rows(g):
                after(pool, silu_done, 3 * g)
                pool.tensor_copy(cacc[:, :, NP:T], prevconv[:, ds(g, 1), :, :]).then_inc(pool_prev, 1)

            def stage(G):
                after(pool, head_done, G)
                pool.tensor_copy(selh[:, :, :], ident[0:VH, ds(2 * G, 2)].unsqueeze(2).broadcast_to([VH, 2, P])
                                 ).then_inc(staged, 1)
                pool.tensor_copy(sc_g[:, :], tab_gc[:, ds(2 * G, 2), :]).then_inc(staged, 1)
                pool.tensor_copy(sc_b[:, :], tab_beta[:, ds(2 * G, 2), :]).then_inc(staged, 1)
                pool.tensor_copy(sc_n[:, :], tab_neg[:, ds(2 * G, 2)]).then_inc(staged, 1)
                pool.tensor_copy(sc_eg[:, :, :], row_eg[:, ds(2 * G, 2), :]).then_inc(staged, 1)
                pool.tensor_copy(sc_eb[:, :, :], tab_eb[:, ds(2 * G, 2), :]).then_inc(staged, 1)
                pool.wait_ge(staged, 6 * G + 6)
                pool.tensor_tensor(NT[:, :, :], bc(strict, 1, 4), sc_b[:, :].unsqueeze(2).broadcast_to([P, 4, P]),
                                   ALU.mult).then_inc(bst_ready, 1)

            def base_blocks(G):
                pool.wait_ge(nt_ready, G + 1)
                pool.tensor_tensor(PaT[:, :, :], NT[:, :, :], bc(base_up, 1, 4), ALU.mult).then_inc(base_ready, 1)
                pool.wait_ge(base_ready, 2 * G + 1)
                pool.tensor_tensor(Um[:, :, :], bc(ident, 1, 4), PaT[:, :, :], ALU.subtract).then_inc(base_ready, 1)

            def decode_pads(G):
                pool.wait_ge(qn_ready, G + 1)
                diag = kq_diag[:, :].rearrange("p (b c) -> p b c", c=P + 1)
                thrice = kv_pad[:, :, :].rearrange("p m (g c) -> p m g c", c=32)[:, :, :, 0:NB]
                k, q = qk[:, 1, NP:T], qk[:, 0, NP:T]
                pool.tensor_tensor(diag[:, :, 0:96:32], k.unsqueeze(2).broadcast_to([P, NB, 3]),
                                   ones[:, 0:3 * NB].rearrange("p (b g) -> p b g", b=NB), ALU.mult
                                   ).then_inc(dec_padded, 1)
                pool.tensor_copy(diag[:, :, 96], q).then_inc(dec_padded, 1)
                pool.tensor_copy(thrice[:, 0, :, :], bc(k, 1, 3)).then_inc(dec_padded, 1)
                for h in range(2):
                    pool.tensor_copy(thrice[:, 1 + h, :, :], bc(vv[:, h, NP:T], 1, 3)).then_inc(dec_padded, 1)

            def decode_keys(G):
                pool.wait_ge(dec_dve, 10 * G + 2)
                pool.tensor_tensor(kmask[:, :, :], bc(dec_kd.bitcast(F32), 1, NB),
                                   sel8[0:96, :].unsqueeze(2).broadcast_to([96, NB, P]),
                                   ALU.mult).then_inc(kmask_ready, 1)

            def turn(g, G):
                for j in range(12):
                    if j == 0 and G is not None:
                        stage(G)
                    if g is not None and j == 0:
                        cached_rows(g)
                    split_lo(pool, chunk(C_IN, 12, g, j + 1) if g is not None else chunk(C_OUT, RAW, 0, j + 1))
                    if j == 1 and G is not None:
                        base_blocks(G)
                    elif j == 2 and G is not None:
                        decode_pads(G)
                    elif j == 8 and G is not None:
                        decode_keys(G)

            pool.wait_ge(lo_ready, C_IN + 1)
            turn(0, None)
            turn(1, 0)
            with pool.Fori(2, GROUPS) as g:
                turn(g, g - 1)
            turn(None, GROUPS - 1)
            pool_after_delta(pool)

        @block.scalar
        def _(act):
            for n in range(TURNS):
                act.wait_ge(prep_pe, n + 1)
                bk = bank[n % 4]
                if n == 0:
                    nc.scalar.activation(gains[:, :], bk[:, 0:6 * KT + 1], ACT.Copy).then_inc(prep_act, 1)
                elif n == 1:
                    nc.scalar.activation(cw_n[:, :, :], bk[:, 0:4 * CT].rearrange("p (j t) -> p j t", j=4),
                                         ACT.Copy).then_inc(prep_act, 1)
                elif n < 6:
                    nc.scalar.activation(scT[:, 16 * (n - 2):16 * (n - 1), :, :], bk[:, 0:16 * 3 * NB], ACT.Copy
                                         ).then_inc(prep_act, 1)
                else:
                    nc.scalar.activation(x_first[:, n - 6, :], bk[:, 0:T], ACT.Copy).then_inc(prep_act, 1)
            act.wait_ge(consts_set, 2)
            first_norm_act(act)
            split_hi(act, chunk(C_BA, RAW, 0, 0))
            split_hi(act, chunk(C_BA, RAW, 0, 1))
            split_hi(act, chunk(C_IN, 12, 0, 0))
            act.wait_ge(w_used, 2)
            nc.scalar.activation(ba[:, 0, :], bank[2][2 * VH:3 * VH, 0:T], ACT.Exp, scale=-1.0).then_inc(ba_act, 1)
            nc.scalar.activation(ba[:, 2, :], bank[2][3 * VH:4 * VH, 0:T], ACT.Copy).then_inc(ba_act, 1)
            act.wait_ge(small_in, 16 * 14)
            nc.scalar.activation(hcol[:, 2:3], hcol[:, 0:1], ACT.Exp).then_inc(ba_act, 1)
            act.wait_ge(ba_dve, 5)
            nc.scalar.activation(ba[:, 5, :], ba[:, 4, :], ACT.Exp).then_inc(ba_act, 1)
            act.wait_ge(ba_act, 4)
            nc.scalar.activation(ba[:, 5, :], ba[:, 5, :], ACT.Ln, bias=ones[0:VH, 0:1]).then_inc(ba_act, 1)
            act.wait_ge(ba_pe, 1)
            nc.scalar.activation(tok_gb[:, :, :, :], bank[3][:, 0:4 * VH], ACT.Copy).then_inc(ba_act, 1)
            act.wait_ge(ba_pe, 3)
            nc.scalar.activation(gc_rows[:, :], bank[0][0:VH, 0:NP], ACT.Copy).then_inc(ba_act, 1)
            nc.scalar.activation(tab_gc[:, :, :], bank[1][:, 0:2 * VH].rearrange("p (c h) -> p h c", c=2),
                                 ACT.Copy).then_inc(ba_act, 1)
            nc.scalar.activation(tab_beta[:, :, :], tok_gb[:, 1, :, :].rearrange("p c h -> p h c"),
                                 ACT.Copy).then_inc(ba_act, 1)
            nc.scalar.activation(tab_neg[:, :], bank[1][:, VH:2 * VH], ACT.Exp).then_inc(ba_act, 1)
            act.wait_ge(ba_pe, 4)
            nc.scalar.activation(row_eg[:, :, :], bank[2][:, 0:VH * NB], ACT.Exp).then_inc(ba_act, 1)
            at = VH * NB
            nc.scalar.activation(tab_eb[:, :, 0], bank[2][:, at:at + VH], ACT.Exp).then_inc(ba_act, 1)
            nc.scalar.activation(tab_eb[:, :, 1], bank[2][:, at + VH:at + 2 * VH], ACT.Copy).then_inc(ba_act, 1)

            def unit_copy(g, u):
                act.wait_ge(w_used, 12 * g + (C_IN + 4 * (u + 1)))
                if u == 0:
                    after(act, conv_out, 2 * g)
                    after(act, st_turned, g)
                if isinstance(g, int) and g == 0:
                    act.wait_ge(pads_set, 1)
                if u == 2:
                    act.wait_ge(silu_done, 3 * g + 2)
                for t in range(2):
                    dst = cacc[:, t, :] if u == 2 else craw[:, 2 * u + t, 3:3 + T]
                    m = nc.scalar.activation(dst, bank[2 * (u % 2) + t][:, 0:T], ACT.Copy)
                m.then_inc(unit_copied, 1)

            def silus(g):
                act.wait_ge(conv_out, 2 * g + 2)
                nc.scalar.activation(qk[:, :, :], cacc[:, 0:2, :], ACT.Silu).then_inc(silu_done, 1)
                nc.scalar.activation(vv[:, :, :], cacc[:, 2:4, :], ACT.Silu).then_inc(silu_done, 1)

            def step(G, n):
                if n == 0:
                    act.wait_ge(unit_copied, 3 * G + 3)
                    after(act, head_done, G)
                    nc.scalar.activation(zs[:, :, :], cacc[:, 0:2, :], ACT.Silu).then_inc(silu_done, 1)
                    nc.scalar.preload_act_table_set("natural_log_exp_and_others")
                    act.wait_ge(st_turned, G + 1)
                    after(act, st_stored, 96 * G)
                    nc.scalar.activation(strow[:, :, :], B[0][0:3 + NB, :], ACT.Copy).then_inc(st_copied, 1)
                elif n == 1:
                    act.wait_ge(ss_ready, G + 1)
                    for i in range(2):
                        nc.scalar.activation(sqn[:, i, :], B[1 + i][:, 0:T], ACT.Ln, bias=bias_c[:, 0:1]
                                             ).then_inc(rn_ln, 1)
                    act.wait_ge(rn_ln, 2 * G + 2)
                    nc.scalar.activation(sqn[:, 0, :], sqn[:, 0, :], ACT.Exp, bias=bias_c[:, 1:2], scale=-0.5
                                         ).then_inc(rn_ready, 1)
                    nc.scalar.activation(sqn[:, 1, :], sqn[:, 1, :], ACT.Exp, scale=-0.5).then_inc(rn_ready, 1)
                    act.wait_ge(v_turned, G + 1)
                    nc.scalar.activation(vtok[:, :, :, :], B[3][:, :], ACT.Copy).then_inc(v_copied, 1)
                elif n == 2:
                    act.wait_ge(k_turned, G + 1)
                    nc.scalar.activation(ktok[:, :, :], B[0][:, 0:2 * P], ACT.Copy).then_inc(k_copied, 1)
                    act.wait_ge(et_pre, 4 * G + 4)
                    nc.scalar.activation(egR[:, :, :], B[1][:, :].rearrange("p (h c n) -> p h c n", h=2, c=2)[
                        :, :, 1, :], ACT.Exp).then_inc(et_exp, 1)
                    nc.scalar.activation(ET[:, :, :], ET[:, :, :], ACT.Exp).then_inc(et_exp, 1)
                    act.wait_ge(et_exp, 3 * G + 2)
                    nc.scalar.activation(sc_e[:, :], ET[:, :, P - 1], ACT.Copy).then_inc(et_exp, 1)
                elif n == 3:
                    act.wait_ge(n_turned, G + 1)
                    nc.scalar.activation(Nm[:, :, :], B[3][:, :], ACT.Copy).then_inc(n_copied, 1)
                elif n in (4, 5, 6, 8):
                    dst, bk = {4: (Pb, 0), 5: (Pa, 2), 6: (Pb, 1), 8: (Tm, 0)}[n]
                    act.wait_ge(inv_pe, 11 * G + (n - 3))
                    nc.scalar.activation(dst[:, :, :], B[bk][:, :], ACT.Copy).then_inc(inv_act, 1)
                elif n == 16:
                    act.wait_ge(seq_pe, 7 * G + 3)
                    nc.scalar.activation(S1[:, :, :], B[3][:, 0:2 * P], ACT.Copy).then_inc(seq_act, 1)
                elif n == 19:
                    act.wait_ge(seq_pe, 7 * G + 6)
                    nc.scalar.activation(oT[:, :, 0:NP], B[2][:, :].rearrange("p (h n) -> p h n", h=2),
                                         ACT.Copy).then_inc(seq_act, 1)
                elif n == 18:
                    act.wait_ge(dec_dve, 10 * G + 6)
                    nc.scalar.activation(dec_dr[:, :, :], dec_d[0:96, :, :], ACT.Copy).then_inc(dec_act, 1)
                elif n == 20:
                    act.wait_ge(dec_pe, 3 * G + 3)
                    nc.scalar.activation(oT[:, :, NP:T], B[1][:, 0:2 * NB].rearrange("p (h b) -> p h b", h=2),
                                         ACT.Copy).then_inc(dec_act, 1)
                elif n == 22:
                    act.wait_ge(on_ss, G + 1)
                    for i in range(2):
                        nc.scalar.activation(sqn[:, i, :], B[i][:, 0:T], ACT.Ln, bias=bias_c[:, 0:1],
                                             scale=1.0 / P).then_inc(on_ln, 1)
                    act.wait_ge(on_ln, 2 * G + 2)
                    nc.scalar.activation(sqn[:, :, :], sqn[:, :, :], ACT.Exp, scale=-0.5).then_inc(on_rn, 1)
                elif n == 23:
                    act.wait_ge(on_gated, G + 1)
                    nc.scalar.activation(o_hi[:, ds(2 * G, 2), :], oT[:, :, :], ACT.Copy).then_inc(on_hi, 1)

            def turn(g, G):
                for j in range(12):
                    split_hi(act, chunk(C_IN, 12, g, j + 1) if g is not None else chunk(C_OUT, RAW, 0, j + 1))
                    if G is not None:
                        step(G, 2 * j)
                    if g is not None and j == 11:
                        silus(g)
                    if G is not None:
                        step(G, 2 * j + 1)
                    if g is not None and j % 4 == 3:
                        unit_copy(g, j // 4)

            turn(0, None)
            turn(1, 0)
            with act.Fori(2, GROUPS) as g:
                turn(g, g - 1)
            state_out(act, GROUPS - 2)
            state_back(act, GROUPS - 1)
            turn(None, GROUPS - 1)
            conv_rows_out(act, GROUPS - 1)
            state_out(act, GROUPS - 1)
            act_after_delta(act)

        @block.tensor
        def _(pe):
            pe.wait_ge(masks_in_s, 16)
            for n in range(TURNS):
                bk = bank[n % 4]
                after(pe, prep_act, n - 3)
                if n == 0:
                    pe.wait_ge(small_in, 16 * 14)
                    m = nc.tensor.transpose(bk[:, 0:6 * KT + 1], rows_in[0:6 * KT + 1, 0, :],
                                            ident[0:6 * KT + 1, 0:6 * KT + 1])
                elif n == 1:
                    for a in range(2):
                        m = nc.tensor.transpose(bk[:, a * P:(a + 1) * P], rows_in[:, 1 + a, :], ident)
                elif n < 6:
                    for i in range(16):
                        t = 16 * (n - 2) + i
                        m = nc.tensor.transpose(bk[:, 3 * NB * i:3 * NB * (i + 1)], sc_rows[:, t * P:(t + 1) * P],
                                                ident[0:3 * NB, 0:3 * NB])
                else:
                    t = n - 6
                    if t == 0:
                        pe.wait_ge(x_in, 32)
                    for b in range(NBLK):
                        nc.tensor.transpose(bk[:, b * P:(b + 1) * P], x_rows[:, b, t * P:(t + 1) * P], ident)
                    m = nc.tensor.transpose(bk[:, NP:T], x_rows_d[:, t * P:(t + 1) * P], ident[0:NB, 0:NB])
                m.then_inc(prep_pe, 1)
            pe.wait_ge(prep_act, TURNS)
            pe.wait_ge(at_in, 32)
            nc.tensor.matmul(bank[4][0:HEADS, 0:3 * WINDOW], relb[:, :], buckets[:, 0:3 * WINDOW], start=True,
                             stop=True).then_inc(at_pe, 1)
            first_norm_pe(pe)
            for j in range(2):
                pe.wait_ge(norm_lo, KT // 2)
                tiles(pe, chunk(C_BA, RAW, 0, j),
                      [(t, 2, h_hi[:, 8 * j + t, :], h_lo[:, 8 * j + t, :], j + t == 0, 8 * j + t == KT - 1)
                       for t in range(8)])
            pe.wait_ge(ba_dve, 7)
            for q_, src in ((0, 6), (1, 1)):
                for c in range(2):
                    at = (2 * q_ + c) * VH
                    m = nc.tensor.transpose(bank[3][:, at:at + VH], ba[:, src, c * P:(c + 1) * P], ident[0:VH, 0:VH])
            m.then_inc(ba_pe, 1)
            pe.wait_ge(ba_act, 6)
            for c in range(2):
                m = nc.tensor.matmul(bank[0][0:VH, c * P:(c + 1) * P], tok_gb[:, 0, c, :], incl, start=True, stop=True)
            m.then_inc(ba_pe, 1)
            nc.tensor.matmul(bank[1][:, 0:2 * VH], incl, tok_gb[:, 0, :, :], start=True, stop=True).then_inc(ba_pe, 1)
            pe.wait_ge(ba_dve, 10)
            nc.tensor.matmul(bank[2][:, 0:VH * NB], ones[0:VH, :], dexp[:, :, :], start=True, stop=True)
            for q_ in range(2):
                at = VH * NB + q_ * VH
                m = nc.tensor.transpose(bank[2][:, at:at + VH], gb_pad[:, q_, :], ident[0:VH, 0:VH])
            m.then_inc(ba_pe, 1)
            pe.wait_ge(ba_act, 13)

            def each4(out, lhsT, rhs_):
                for m_ in range(4):
                    mm = nc.tensor.matmul(out[:, m_ * P:(m_ + 1) * P], lhsT[:, m_, :], rhs_[:, m_, :],
                                          start=True, stop=True)
                return mm

            def step(G, n):
                inv = lambda s, k: pe.wait_ge(s, (4 if s is inv_act else 13) * G + k)
                if n == 0:
                    after(pe, on_ln, 2 * G)
                    pe.wait_ge(unit_copied, 3 * G + 2)
                    for t in range(4):
                        m = nc.tensor.transpose(B[0][0:3 + NB, t * P:(t + 1) * P], craw[:, t, NP:NP + 3 + NB], ident)
                    m.then_inc(st_turned, 1)
                elif n == 1:
                    pe.wait_ge(sq_ready, G + 1)
                    for i in range(2):
                        m = nc.tensor.matmul(B[1 + i][:, 0:T], ones, sqn[:, i, :], start=True, stop=True)
                    m.then_inc(ss_ready, 1)
                    pe.wait_ge(silu_done, 3 * G + 2)
                    for h in range(2):
                        for c in range(2):
                            at = (2 * h + c) * P
                            m = nc.tensor.transpose(B[3][:, at:at + P], vv[:, h, c * P:(c + 1) * P], ident)
                    m.then_inc(v_turned, 1)
                elif n == 2:
                    pe.wait_ge(rn_ready, 2 * G + 2)
                    pe.wait_ge(staged, 6 * G + 6)
                    for h in range(2):
                        m = nc.tensor.matmul(B[1][:, h * NP:(h + 1) * NP], selh[:, h, :], gc_rows[:, :],
                                             start=True, stop=True)
                    m.then_inc(gc_spread, 1)
                    pe.wait_ge(qn_ready, G + 1)
                    pe.wait_ge(st_copied, G + 1)
                    for c in range(2):
                        m = nc.tensor.transpose(B[0][:, c * P:(c + 1) * P], qk[:, 1, c * P:(c + 1) * P], ident)
                    m.then_inc(k_turned, 1)
                    for i, src in ((0, 1), (1, 0)):
                        for c in range(2):
                            at = (2 * i + c) * P
                            m = nc.tensor.matmul(B[2][:, at:at + P], qk[:, 1, c * P:(c + 1) * P],
                                                 qk[:, src, c * P:(c + 1) * P], start=True, stop=True)
                    m.then_inc(kq_ready, 1)
                elif n == 3:
                    pe.wait_ge(nt_ready, G + 1)
                    pe.wait_ge(v_copied, G + 1)
                    for m_ in range(4):
                        m = nc.tensor.transpose(B[3][:, m_ * P:(m_ + 1) * P], NT[:, m_, :], ident)
                    m.then_inc(n_turned, 1)
                elif n == 4:
                    pe.wait_ge(base_ready, 2 * G + 1)
                    pe.wait_ge(pa_ready, G + 1)
                    each4(B[0], PaT, Pa)
                    each4(B[1], Pa, PaT).then_inc(inv_pe, 1)
                elif n == 5:
                    inv(inv_act, 1)
                    inv(inv_dve, 1)
                    pe.wait_ge(base_ready, 2 * G + 2)
                    each4(B[2], PbT, Pb)
                    each4(B[3], Pb, PbT)
                    each4(B[0], Pb, Um).then_inc(inv_pe, 1)
                elif n == 6:
                    inv(inv_act, 2)
                    inv(inv_dve, 3)
                    each4(B[1], PaT, Pa)
                    each4(B[2], Pa, Um).then_inc(inv_pe, 1)
                elif n == 7:
                    inv(inv_act, 3)
                    inv(inv_dve, 4)
                    each4(B[3], Pb, Um).then_inc(inv_pe, 1)
                elif n == 8:
                    inv(inv_dve, 5)
                    for m_ in range(4):
                        m = nc.tensor.transpose(B[0][:, m_ * P:(m_ + 1) * P], Um[:, m_, :], ident)
                    m.then_inc(inv_pe, 1)
                elif n == 9:
                    inv(inv_dve, 5)
                    each4(B[1], Nm, Um).then_inc(inv_pe, 1)
                elif n == 10:
                    inv(inv_act, 4)
                    inv(inv_dve, 6)
                    each4(B[2], Tm, Xm)
                    each4(B[3], Xm, Tm).then_inc(inv_pe, 1)
                elif n == 11:
                    inv(inv_dve, 8)
                    each4(B[0], Nm, Um).then_inc(inv_pe, 1)
                elif n == 12:
                    inv(inv_dve, 9)
                    each4(B[1], Tm, Xm)
                    each4(B[2], Xm, Tm).then_inc(inv_pe, 1)
                elif n == 13:
                    inv(inv_dve, 11)
                    each4(B[3], Nm, Um).then_inc(inv_pe, 1)
                elif n == 14:
                    inv(inv_dve, 12)
                    each4(B[0], Tm, Xm).then_inc(inv_pe, 1)
                elif n == 15:
                    inv(inv_dve, 13)
                    for h in range(2):
                        m = nc.tensor.matmul(B[1][:, h * P:(h + 1) * P], Um[:, 2 * h, :], vtok[:, h, 0, :],
                                             start=True, stop=True)
                    m.then_inc(seq_pe, 1)
                    pe.wait_ge(dec_padded, 5 * G + 5)
                    for i in range(3):
                        nc.tensor.transpose(B[0][0:96, i * P:(i + 1) * P], kv_pad[:, i, :], ident)
                    nc.tensor.matmul(B[0][0:96, 3 * P:3 * P + NB], kv_pad[:, 0, :], qk[:, 0, NP:T], start=True,
                                     stop=True).then_inc(dec_pe, 1)
                elif n == 16:
                    pe.wait_ge(seq_dve, 7 * G + 1)
                    for h in range(2):
                        m = nc.tensor.matmul(B[2][:, h * NP:h * NP + P], vn[:, h, :], intraT[:, 2 * h, :],
                                             start=True, stop=True)
                    m.then_inc(seq_pe, 1)
                    pe.wait_ge(seq_dve, 7 * G + 2)
                    pe.wait_ge(k_copied, G + 1)
                    nc.tensor.matmul(B[3][:, 0:2 * P], ktok[:, 0, :], vn2[:, :, :], start=True,
                                     stop=True).then_inc(seq_pe, 1)
                elif n == 17:
                    pe.wait_ge(seq_act, 2 * G + 1)
                    pe.wait_ge(dec_dve, 10 * G + 4)
                    nc.tensor.matmul(B[0][:, 0:2 * P], qk[:, 1, P:2 * P], S1[:, :, :], start=True,
                                     stop=True).then_inc(seq_pe, 1)
                    pe.wait_ge(s_loaded, 32 * G + 32)
                    for b in range(NB):
                        m = nc.tensor.matmul(B[1][:, 0:2 * P], kq_diag[:, b * P:(b + 1) * P], s_dec[:, :, b, :],
                                             start=(b == 0), stop=(b == NB - 1))
                    m.then_inc(dec_pe, 1)
                elif n == 18:
                    pe.wait_ge(seq_dve, 7 * G + 4)
                    for h in range(2):
                        m = nc.tensor.matmul(B[0][:, h * P:(h + 1) * P], Um[:, 2 * h + 1, :], rhs[:, h, :],
                                             start=True, stop=True)
                    m.then_inc(seq_pe, 1)
                elif n == 19:
                    pe.wait_ge(seq_dve, 7 * G + 5)
                    pe.wait_ge(qdec_ready, G + 1)
                    for h in range(2):
                        out = B[2][:, h * NP + P:(h + 1) * NP]
                        nc.tensor.matmul(out, S1[:, h, :], qdec[:, h, :], start=True, stop=False)
                        m = nc.tensor.matmul(out, vn[:, h, :], intraT[:, 2 * h + 1, :], start=False, stop=True)
                    m.then_inc(seq_pe, 1)
                    pe.wait_ge(seq_dve, 7 * G + 6)
                    nc.tensor.matmul(B[3][:, 0:2 * P], ktok[:, 1, :], vn2[:, :, :], start=True,
                                     stop=True).then_inc(seq_pe, 1)
                elif n == 20:
                    pe.wait_ge(dec_dve, 10 * G + 9)
                    for h in range(2):
                        m = nc.tensor.matmul(B[1][:, h * NB:(h + 1) * NB], dec_d[:, h, :], dec_sel[:, h, :],
                                             start=True, stop=True)
                    m.then_inc(dec_pe, 1)
                elif n in (21, 22):
                    if n == 21:
                        pe.wait_ge(kmask_ready, G + 1)
                        pe.wait_ge(dec_dve, 10 * G + 10)
                        pe.wait_ge(seq_act, 2 * G + 2)
                        pe.wait_ge(seq_dve, 7 * G + 7)
                    else:
                        pe.wait_ge(on_sq, G + 1)
                        for i in range(2):
                            m = nc.tensor.matmul(B[i][:, 0:T], ones, sqn[:, i, :], start=True, stop=True)
                        m.then_inc(on_ss, 1)
                    for i in range(2 * (n - 21), 2 * (n - 21) + 2):
                        if i >= 2:
                            pe.wait_ge(outer_dve, 16 * G + 4 * (i - 1))
                        for bb in range(2):
                            m = nc.tensor.matmul(B[2 + i % 2][:, bb * 2 * P:(bb + 1) * 2 * P],
                                                 kmask[:, 2 * i + bb, :], dec_dr[:, :, :], start=True, stop=True)
                        m.then_inc(outer_pe, 1)

            def turn(g, G):
                for j in range(12):
                    u, k = j // 4, 4 * (j % 4)
                    tl = [(2 * kk + n if u else 4 * n + kk, 2 * (u % 2) + n, h_hi[:, k + kk, :], h_lo[:, k + kk, :],
                           k + kk == 0, k + kk == KT - 1) for kk in range(4) for n in range(2)]
                    if G is not None:
                        step(G, 2 * j)
                    if g is None:
                        if j == 0:
                            pe.wait_ge(unit_copied, 3 * GROUPS)
                        if j == 11:
                            pe.wait_ge(head_done, GROUPS - 1)
                        tl = [(4 * kk + n, n, o_hi[:, 2 * j + kk, :], o_lo[:, 2 * j + kk, :], j + kk == 0, False)
                              for kk in range(2) for n in range(4)]
                        tiles(pe, chunk(C_OUT, RAW, 0, j), tl[0:4], 0)
                    else:
                        if j == 0:
                            after(pe, unit_copied, 3 * g)
                        elif j == 8:
                            pe.wait_ge(unit_copied, 3 * g + 1)
                        tiles(pe, chunk(C_IN, 12, g, j), tl[0:4], 0)
                    if G is not None:
                        step(G, 2 * j + 1)
                    tiles(pe, chunk(C_IN, 12, g, j) if g is not None else chunk(C_OUT, RAW, 0, j), tl[4:8], 1)

            turn(0, None)
            turn(1, 0)
            with pe.Fori(2, GROUPS) as g:
                turn(g, g - 1)
            turn(None, GROUPS - 1)
            pe_after_delta(pe)
        @block.vector
        def _(dve):
            tt, ts, stt = nc.vector.tensor_tensor, nc.vector.tensor_scalar, nc.vector.scalar_tensor_tensor
            dve.wait_ge(prep_act, 6)
            tap = lambda j: cw_n[:, j, :].unsqueeze(2).broadcast_to([P, CT, NB])
            tt(pc_a[:, :, :], scT[:, :, :, 0], tap(0), ALU.mult).then_inc(prep_dve, 1)
            tt(pc_b[:, :, :], scT[:, :, :, 1], tap(1), ALU.mult).then_inc(prep_dve, 1)
            dve.wait_ge(prep_dve, 2)
            tt(pc_a[:, :, :], pc_a[:, :, :], pc_b[:, :, :], ALU.add).then_inc(prep_dve, 1)
            dve.wait_ge(prep_dve, 3)
            tt(pc_b[:, :, :], scT[:, :, :, 2], tap(2), ALU.mult).then_inc(prep_dve, 1)
            dve.wait_ge(prep_dve, 4)
            tt(pc_a[:, :, :], pc_a[:, :, :], pc_b[:, :, :], ALU.add).then_inc(prep_dve, 1)
            dve.wait_ge(prep_dve, 5)
            for t, sel in enumerate((slice(0, KT), slice(KT, 2 * KT), slice(2 * KT, CT, 2), slice(2 * KT + 1, CT, 2))):
                nc.vector.tensor_copy(convw[:, :, t, :], cw_n[:, :, sel].rearrange("p j g -> p g j")
                                      ).then_inc(prep_dve, 1)
                nc.vector.tensor_copy(prevconv[:, :, t, :], pc_a[:, sel, :]).then_inc(prep_dve, 1)
            dve.wait_ge(at_pe, 1)
            tt(brow[:, :], bank[4][0:HEADS, 0:3 * WINDOW], buckets[:, 3 * WINDOW:6 * WINDOW], ALU.add).then_inc(at_brow, 1)
            first_norm_dve(dve)
            split_lo(dve, chunk(C_BA, RAW, 0, 0))
            split_lo(dve, chunk(C_BA, RAW, 0, 1))
            dve.wait_ge(ba_act, 1)
            ts(ba[:, 3, :], ba[:, 0, :], 1.0, None, ALU.add).then_inc(ba_dve, 1)
            dve.wait_ge(ba_dve, 1)
            nc.vector.reciprocal(ba[:, 1, :], ba[:, 3, :]).then_inc(ba_dve, 1)
            dve.wait_ge(ba_act, 3)
            ts(ba[:, 2, :], ba[:, 2, :], hcol[:, 1:2], None, ALU.add).then_inc(ba_dve, 1)
            dve.wait_ge(ba_dve, 3)
            ts(ba[:, 7, :], ba[:, 2, :], 0.0, None, ALU.max).then_inc(ba_dve, 1)
            dve.wait_ge(ba_dve, 4)
            stt(ba[:, 4, :], ba[:, 7, :], -2.0, ba[:, 2, :], ALU.mult, ALU.add).then_inc(ba_dve, 1)
            dve.wait_ge(ba_act, 5)
            tt(ba[:, 0, :], ba[:, 7, :], ba[:, 5, :], ALU.add).then_inc(ba_dve, 1)
            dve.wait_ge(ba_dve, 6)
            ts(ba[:, 6, :], ba[:, 0, :], hcol[:, 2:3], -1.0, ALU.mult, ALU.mult).then_inc(ba_dve, 1)
            dve.wait_ge(ba_dve, 7)
            eye = ident[0:VH, 0:VH].unsqueeze(2).broadcast_to([VH, VH, NB])
            tt(dexp[:, :, :], bc(ba[:, 6, NP:T], 1, VH), eye, ALU.mult).then_inc(ba_dve, 1)
            dve.wait_ge(consts_set, 3)
            for q_, src in ((0, 6), (1, 1)):
                nc.vector.tensor_copy(gb_pad[:, q_, :].rearrange("p (g c) -> p g c", c=32)[:, :, 0:NB],
                                      bc(ba[:, src, NP:T], 1, 4)).then_inc(ba_dve, 1)
            dve.wait_ge(ba_act, 13)
            ts(tab_neg[:, :], tab_neg[:, :], -1.0, None, ALU.mult).then_inc(tables_done, 1)
            stt(tab_eb[:, :, 2], tab_eb[:, :, 0], -1.0, tab_eb[:, :, 1], ALU.mult, ALU.mult).then_inc(tables_done, 1)
            split_lo(dve, chunk(C_IN, 12, 0, 0))

            def conv(g, u, k):
                j, t = k // 2, 2 * u + k % 2
                if k == 0:
                    dve.wait_ge(unit_copied, 3 * g + (u + 1))
                    after(dve, silu_done, 3 * g)
                if k == 6:
                    dve.wait_ge(pool_prev, g + 1)
                w = convw[:, ds(g, 1), t, j]
                if j == 0:
                    m = ts(cacc[:, t, 0:NP], craw[:, t, 0:NP], w, None, ALU.mult)
                else:
                    n = T if j == 3 else NP
                    dve.wait_ge(conv_step, 14 * g + 7 * u + 2 * (j - 1) + (t % 2) + 1)
                    m = stt(cacc[:, t, 0:n], craw[:, t, j:j + n], w, cacc[:, t, 0:n], ALU.mult, ALU.add)
                m.then_inc(conv_out if k == 7 else conv_step, 1)

            def step(G, n):
                c2 = lambda ap: ap.rearrange("p (c n) -> p c n", c=2).unsqueeze(1).broadcast_to([P, 2, 2, P])
                hc = lambda ap: ap.rearrange("p (h c) n -> p h c n", h=2)
                h2 = lambda ap: ap.rearrange("p (h n) -> p h n", h=2)
                m4 = lambda ap: ap.rearrange("p (m n) -> p m n", m=4)
                if n == 0:
                    dve.wait_ge(silu_done, 3 * G + 1)
                    tt(sqn[:, :, :], qk[:, :, :], qk[:, :, :], ALU.mult).then_inc(sq_ready, 1)
                elif n == 1:
                    dve.wait_ge(rn_ready, 2 * G + 2)
                    tt(qk[:, :, :], qk[:, :, :], sqn[:, :, :], ALU.mult).then_inc(qn_ready, 1)
                elif n == 2:
                    dve.wait_ge(gc_spread, G + 1)
                    for m_ in range(4):
                        ts(ET[:, m_, :], B[1][:, m_ * P:(m_ + 1) * P], sc_g[:, m_:m_ + 1], 0.0, ALU.subtract,
                           ALU.min).then_inc(et_pre, 1)
                    dve.wait_ge(kq_ready, G + 1)
                    dve.wait_ge(bst_ready, G + 1)
                    tt(hc(NT[:, :, :]), c2(B[2][:, 0:2 * P]), hc(NT[:, :, :]), ALU.mult).then_inc(kk_ready, 1)
                    tt(hc(intraT[:, :, :]), c2(B[2][:, 2 * P:4 * P]), hc(bc(incl, 1, 4)), ALU.mult).then_inc(kk_ready, 1)
                    dve.wait_ge(et_exp, 3 * G + 3)
                    dve.wait_ge(kk_ready, 2 * G + 2)
                    tt(NT[:, :, :], NT[:, :, :], ET[:, :, :], ALU.mult).then_inc(nt_ready, 1)
                    tt(intraT[:, :, :], intraT[:, :, :], ET[:, :, :], ALU.mult).then_inc(intra_ready, 1)
                    dve.wait_ge(qn_ready, G + 1)
                    tt(qdec[:, :, :], bc(qk[:, 0, P:2 * P], 1, 2), egR[:, :, :], ALU.mult).then_inc(qdec_ready, 1)
                elif n == 3:
                    dve.wait_ge(n_copied, G + 1)
                    tt(Pa[:, :, :], Nm[:, :, :], bc(base_lo, 1, 4), ALU.mult).then_inc(pa_ready, 1)
                elif 4 <= n <= 14:
                    if n != 8:
                        dve.wait_ge(inv_pe, 11 * G + (n - 3))
                    own = lambda k: dve.wait_ge(inv_dve, 13 * G + k)
                    add = lambda dst, bk, op: tt(dst[:, :, :], dst[:, :, :], m4(B[bk][:, :]), op).then_inc(inv_dve, 1)
                    msk = lambda bk, lv: tt(Xm[:, :, :], m4(B[bk][:, :]), bc(lv, 1, 4), ALU.mult).then_inc(inv_dve, 1)
                    if n == 4:
                        nc.vector.tensor_copy(PbT[:, :, :], m4(B[1][:, :])).then_inc(inv_dve, 1)
                    elif n == 5:
                        nc.vector.tensor_copy(PaT[:, :, :], m4(B[3][:, :])).then_inc(inv_dve, 1)
                        add(Um, 0, ALU.add)
                    elif n == 6:
                        own(3)
                        add(Um, 2, ALU.add)
                    elif n == 7:
                        own(4)
                        add(Um, 3, ALU.add)
                    elif n == 9:
                        msk(1, lvl16)
                    elif n == 10:
                        own(5)
                        add(Um, 2, ALU.subtract)
                        add(Tm, 3, ALU.subtract)
                    elif n == 11:
                        msk(0, lvl32)
                    elif n == 12:
                        own(8)
                        add(Um, 1, ALU.subtract)
                        add(Tm, 2, ALU.subtract)
                    elif n == 13:
                        msk(3, lvl64)
                    elif n == 14:
                        own(10)
                        add(Um, 0, ALU.subtract)
                elif n in (15, 18):
                    c, k = (0, 1) if n == 15 else (1, 5)
                    dve.wait_ge(seq_pe, 7 * G + k)
                    col = lambda s: s[:, c::2].unsqueeze(2).broadcast_to([P, 2, P])
                    tt(vn[:, :, :], h2(B[1 - c][:, 0:2 * P]), col(sc_b), ALU.mult).then_inc(seq_dve, 1)
                    dve.wait_ge(seq_dve, 7 * G + k)
                    tt(vn2[:, :, :], vn[:, :, :], col(sc_e), ALU.mult).then_inc(seq_dve, 1)
                    if n == 18:
                        dve.wait_ge(dec_act, 2 * G + 1)
                        mid = dec_dr[32:64]
                        tt(mid, dec_d[32:64, :, :], mid.bitcast(F32), ALU.subtract).then_inc(dec_dve, 1)
                elif n == 16:
                    dve.wait_ge(dec_pe, 3 * G + 1)
                    nc.vector.tensor_copy(dec_kd, B[0][0:96, 0:P]).then_inc(dec_dve, 1)
                    dve.wait_ge(dec_dve, 10 * G + 1)
                    tt(dec_kd[64:96], B[0][64:96, 0:P], dec_kd[64:96].bitcast(F32), ALU.subtract).then_inc(dec_dve, 1)
                    tt(dec_d[0:96, :, :], h2(B[0][0:96, P:3 * P]), sc_eb[0:96, :, 1].unsqueeze(2).broadcast_to([96, 2, P]),
                       ALU.mult).then_inc(dec_dve, 1)
                    tt(dec_qk[0:96, :], B[0][0:96, 3 * P:3 * P + NB], ident[0:96, 0:NB], ALU.mult).then_inc(dec_dve, 1)
                elif n == 17:
                    dve.wait_ge(seq_pe, 7 * G + 4)
                    for h in range(2):
                        stt(rhs[:, h, :], B[0][:, h * P:(h + 1) * P], sc_n[:, h:h + 1], vtok[:, h, 1, :],
                            ALU.mult, ALU.add).then_inc(seq_dve, 1)
                    dve.wait_ge(dec_pe, 3 * G + 2)
                    dve.wait_ge(dec_dve, 10 * G + 4)
                    for h in range(2):
                        stt(dec_d[0:96, h, :], B[1][0:96, h * P:(h + 1) * P], sc_eb[0:96, h, 2:3], dec_d[0:96, h, :],
                            ALU.mult, ALU.add).then_inc(dec_dve, 1)
                    nc.vector.tensor_copy(dec_d[96:P, :, :], h2(B[1][96:P, 0:2 * P])).then_inc(dec_dve, 1)
                    for h in range(2):
                        stt(dec_sel[:, h, :], ident[:, 96:96 + NB], sc_eb[:, h, 0:1], dec_qk[:, :], ALU.mult,
                            ALU.add).then_inc(dec_dve, 1)
                elif n == 19:
                    dve.wait_ge(seq_pe, 7 * G + 7)
                    after(dve, prompt_state_stored, 16 * G)
                    for h in range(2):
                        m = stt(S2[:, h, :], S1[:, h, :], egR[:, h, P - 1:P], B[3][:, h * P:(h + 1) * P],
                                ALU.mult, ALU.add)
                    m.then_inc(seq_dve, 1)
                elif n in (21, 22):
                    if n == 21:
                        dve.wait_ge(seq_act, 2 * G + 2)
                        dve.wait_ge(dec_act, 2 * G + 2)
                        tt(sqn[:, :, :], oT[:, :, :], oT[:, :, :], ALU.mult).then_inc(on_sq, 1)
                    for i in range(2 * (n - 21), 2 * (n - 21) + 2):
                        dve.wait_ge(outer_pe, 4 * G + (i + 1))
                        for bb in range(2):
                            for h in range(2):
                                s = s_dec[:, h, 2 * i + bb, :]
                                at = (2 * bb + h) * P
                                stt(s, s, sc_eg[:, h, 2 * i + bb:2 * i + bb + 1], B[2 + i % 2][:, at:at + P],
                                    ALU.mult, ALU.add).then_inc(outer_dve, 1)
                elif n == 23:
                    dve.wait_ge(on_rn, G + 1)
                    stt(oT[:, :, :], oT[:, :, :], gains[:, 6 * KT:6 * KT + 1], sqn[:, :, :], ALU.mult,
                        ALU.mult).then_inc(on_scaled, 1)
                    dve.wait_ge(on_scaled, G + 1)
                    dve.wait_ge(silu_done, 3 * G + 3)
                    tt(oT[:, :, :], oT[:, :, :], zs[:, :, :], ALU.mult).then_inc(on_gated, 1)
                    dve.wait_ge(on_hi, G + 1)
                    tt(o_lo[:, ds(2 * G, 2), :], oT[:, :, :], o_hi[:, ds(2 * G, 2), :].bitcast(F32),
                       ALU.subtract).then_inc(head_done, 1)

            def turn(g, G):
                for j in range(12):
                    for n in (2 * j, 2 * j + 1):
                        if G is not None:
                            step(G, n)
                        if g is not None and 8 <= n < 22:
                            conv(g, (n - 8) // 8, (n - 8) % 8)
                        elif g is not None and n == 22:
                            conv(g, 1, 6)
                            conv(g, 1, 7)

            turn(0, None)
            turn(1, 0)
            with dve.Fori(2, GROUPS) as g:
                turn(g, g - 1)
            turn(None, GROUPS - 1)

            def add_columns(base, per, U0, k, last=False, done=0):
                def once(i, final=False, done=0):
                    for j in range(done, 2 * per):
                        if not (final and j == 2 * per - 1):
                            split_lo(dve, chunk(base, 2 * per, i, j + 1))
                        if j == per + 1:
                            part_unit(dve, k, 2 * i)
                        if j % per == per - 1:
                            u = j // per
                            dve.wait_ge(w_used, 2 * per * i + (base + per * (u + 1)))
                            if done and u == 0:
                                dve.wait_ge(x_back, 16)
                            for n in range(4):
                                x = x_res[:, ds(8 * i + 4 * u + n, 1), :]
                                m = tt(x, x, bank[4 * u + n][:, 0:T].unsqueeze(1), ALU.add)
                            m.then_inc(u_read, 1)
                            if u:
                                part_unit(dve, k, 2 * i + 1)
                if last or done:
                    once(0, done=done)
                    once(1, last)
                else:
                    with dve.Fori(0, 2) as i:
                        once(i)

            def ffn(l):
                per, which = UNIT["gu"], f"ffn{l}"

                def hidden(n, u):
                    dve.wait_ge(f_silued, n + (FT // 2 * l + 1))
                    for t in range(2):
                        m = tt(f_h[:, t, :], f_silu[:, t, :], bank[4 * u + 2 + t][:, 0:T], ALU.mult)
                    m.then_inc(u_read, 1)

                def hidden_lo(n):
                    dve.wait_ge(f_hi, n + (FT // 2 * l + 1))
                    tt(a_lo[:, ds(2 * n, 2), :], f_h[:, :, :], a_hi[:, ds(2 * n, 2), :].bitcast(F32),
                       ALU.subtract).then_inc(f_lo, 1)

                def once(i, first=False):
                    for j in range(2 * per):
                        if first and j < PAIRS:
                            lo_pair(dve, which, j)
                        if not (first and j < PAIRS):
                            if first and j == PAIRS:
                                dve.wait_ge(lo_ready, C_GU[l] + PAIRS + 1)
                            split_lo(dve, chunk(C_GU[l], 2 * per, i, j + 1))
                        if first and j + 1 < PAIRS:
                            scale_pair(dve, which, j + 1)
                        if j == 0 and not first:
                            hidden(2 * i - 1, 1)
                        elif j == 1 and not first:
                            hidden_lo(2 * i - 1)
                        elif j == per:
                            hidden(2 * i, 0)
                        elif j == per + 1:
                            hidden_lo(2 * i)
                once(0, True)
                with dve.Fori(1, FT // 4) as i:
                    once(i)
                hidden(FT // 2 - 1, 1)
                hidden_lo(FT // 2 - 1)
                add_columns(C_DOWN[l], UNIT["down"], U_DOWN[l], 2 * l + 1, last=l == 1)

            dve.wait_ge(head_done, GROUPS)
            nc.vector.memset(dec_sel[:, 0, :], 0.0).then_inc(u_read, 1)
            nc.vector.memset(dec_sel[:, 1, :], 0.0).then_inc(u_read, 1)
            dve.wait_ge(lo_ready, C_OUT + 13)
            add_columns(C_OUT, UNIT["out"], U_OUT, 0, done=12)
            norm_dve(dve, "ffn0")
            ffn(0)
            norm_dve(dve, "kv")
            for j in range(UNIT["kv"]):
                lo_pair(dve, "kv", j)
                scale_pair(dve, *(("kv", j + 1) if j + 1 < PAIRS else ("mix1", 0)))
            for j in range(4 * UNIT["q"]):
                if j < PAIRS:
                    lo_pair(dve, "mix1", j)
                if j >= PAIRS:
                    if j == PAIRS:
                        dve.wait_ge(lo_ready, C_Q + PAIRS + 1)
                    split_lo(dve, chunk(C_Q, RAW, 0, j + 1))
                if j + 1 < PAIRS:
                    scale_pair(dve, "mix1", j + 1)

            dve.wait_ge(d_pe, 4)
            dve.wait_ge(bias_in, 16 * 8)
            for t in range(2):
                stt(sdc[:, t, :], bank[0][:, t * WINDOW:(t + 1) * WINDOW], 1.0, bias_d[:, :], ALU.mult,
                    ALU.add).then_inc(d_dve, 1)
            dve.wait_ge(d_dve, 2)
            nc.vector.tensor_reduce(dmx[:, :], sdc[:, :, :], AX.X, ALU.max).then_inc(d_dve, 1)
            dve.wait_ge(d_dve, 3)
            ts(dmx[:, :], dmx[:, :], sink_d[:, 0:1], None, ALU.max).then_inc(d_dve, 1)
            dve.wait_ge(d_dve, 4)
            ts(dnm[:, :], dmx[:, :], -1.0, None, ALU.mult).then_inc(d_dve, 1)
            dve.wait_ge(d_dve, 5)
            ts(des[:, :], dnm[:, :], sink_d[:, 0:1], None, ALU.add).then_inc(d_dve, 1)
            dve.wait_ge(d_act, 9)
            tt(drec[:, :], dsum[:, :], des[:, :], ALU.add).then_inc(d_dve, 1)
            dve.wait_ge(d_dve, 7)
            nc.vector.reciprocal(drec[:, :], drec[:, :]).then_inc(d_dve, 1)
            dve.wait_ge(d_dve, 8)
            tt(sdc[:, :, :], sdc[:, :, :], drec[:, :].unsqueeze(2).broadcast_to([P, 2, WINDOW]), ALU.mult).then_inc(d_dve, 1)
            dve.wait_ge(d_act, 12)
            tt(ao_lo[:, :, NP:T], od[:, :, :], ao_hi[:, :, NP:T].bitcast(F32), ALU.subtract).then_inc(d_dve, 1)

            def maxima(kv, p):
                n = 4 * kv + p
                b = p % 2
                dve.wait_ge(p_s, n + 1)
                if p == 0:
                    dve.wait_ge(bias_in, 16 * kv + 16 * 9)
                if p >= 2 or not isinstance(kv, int) or kv:
                    dve.wait_ge(p_turn, n - 1)
                for h in range(2):
                    s = bank[2 * b + h]
                    stt(scores_sb[:, b, h, 0:256], s[:, 0:256], ATT, bias[:, 2 * p + h, :], ALU.mult,
                        ALU.add).then_inc(p_add, 1)
                    stt(scores_sb[:, b, h, 256:384], s[:, 256:384], ATT, bias[:, 2 * p + h, 128:256], ALU.mult,
                        ALU.add).then_inc(p_add, 1)
                dve.wait_ge(p_add, 4 * n + 4)
                nc.vector.tensor_reduce(smx[:, b, 0:2], scores_sb[:, b, :, 0:256], AX.X, ALU.max).then_inc(p_max, 1)
                nc.vector.tensor_reduce(smx[:, b, 2:4], scores_sb[:, b, :, 256:384], AX.X, ALU.max).then_inc(p_max, 1)
                dve.wait_ge(p_max, 5 * n + 2)
                sk = bc(sink_st[:, 2 * p:2 * p + 2], 1, 2)
                v22 = lambda ap: ap.rearrange("p (k h) -> p k h", k=2)
                tt(v22(smx[:, b, :]), v22(smx[:, b, :]), sk, ALU.max).then_inc(p_max, 1)
                dve.wait_ge(p_max, 5 * n + 3)
                ts(snm[:, b, :], smx[:, b, :], -1.0, None, ALU.mult).then_inc(p_max, 1)
                dve.wait_ge(p_max, 5 * n + 4)
                tt(v22(ses[:, b, :]), v22(snm[:, b, :]), sk, ALU.add).then_inc(p_max, 1)

            def attend(kv):
                for p in range(4):
                    n = 4 * kv + p
                    b = p % 2
                    if p % 2 == 0:
                        maxima(kv, p)
                        maxima(kv, p + 1)
                    dve.wait_ge(p_exp, 5 * n + 5)
                    tt(srec[:, b, :], ssum[:, b, :], ses[:, b, :], ALU.add).then_inc(p_den, 1)
                    dve.wait_ge(p_den, 2 * n + 1)
                    nc.vector.reciprocal(srec[:, b, :], srec[:, b, :]).then_inc(p_den, 1)
                    dve.wait_ge(p_den, 2 * n + 2)
                    for k, (a, e) in enumerate(((0, 256), (256, 384))):
                        tt(scores_sb[:, b, :, a:e], scores_sb[:, b, :, a:e],
                           srec[:, b, 2 * k:2 * k + 2].unsqueeze(2).broadcast_to([P, 2, e - a]), ALU.mult
                           ).then_inc(p_norm, 1)
                dve.wait_ge(p_hi, kv + 1)
                tt(ao_lo[:, ds(4 * kv, 4), 0:NP], o_st[:, :, :], ao_hi[:, ds(4 * kv, 4), 0:NP].bitcast(F32),
                   ALU.subtract).then_inc(p_lo, 1)

            attend(0)
            with dve.Fori(1, KV) as kv:
                attend(kv)
            add_columns(C_O, UNIT["o"], U_O, 2)
            norm_dve(dve, "ffn1")
            ffn(1)
            norm_dve(dve, "final")
            for t in range(KT):
                if t >= 2:
                    dve.wait_ge(y_turned, t - 1)
                stt(norm_h[:, t % 2, :], x_res[:, t, :], gains[:, 5 * KT + t:5 * KT + t + 1], rstd[:, :], ALU.mult,
                    ALU.mult).then_inc(norm_scaled, 1)

_INS = ["x_prompt", "x_sample", "state_delta", "state_conv", "cache_k_win", "cache_v_win", "norm_mix", "norm_ffn",
        "w_in_a", "conv_w_a", "a_log", "dt_bias", "gnorm_a", "w_out_a", "norm_kv", "w_kv", "w_q_b", "w_o_b",
        "sinks", "rel_bias", "w_gate_up", "w_down", "norm_final"]


def kernel(**inputs):
    import concourse.bacc as _bacc
    from concourse.bass_utils import run_bass_kernel_spmd as _run

    nc = _bacc.Bacc("TRN2", target_bir_lowering=False, num_devices=1)
    masks, buckets = shape_constants()
    given = [(name, np.ascontiguousarray(inputs[name])) for name in _INS] + [("masks", masks), ("buckets", buckets)]
    arrays, args = {}, []
    for name, a in given:
        arrays[f"in_{name}_dram"] = a
        args.append(nc.dram_tensor(f"in_{name}_dram", a.shape, mybir.dt.from_np(a.dtype), kind="ExternalInput").ap())
    win = (inputs["cache_k_win"].shape[1:])
    batch = inputs["x_prompt"].shape[0]
    sd, sc = inputs["state_delta"].shape, inputs["state_conv"].shape
    outs = [inputs["x_prompt"].shape, inputs["x_sample"].shape, (sd[0], batch) + tuple(sd[2:]),
            (sc[0], batch) + tuple(sc[2:]), (batch,) + tuple(win), (batch,) + tuple(win), sd, sc,
            inputs["cache_k_win"].shape, inputs["cache_v_win"].shape]
    for i, shape in enumerate(outs):
        args.append(nc.dram_tensor(f"out_{i}_dram", tuple(shape), F32, kind="ExternalOutput").ap())
    yoco_step(nc, *args)
    r = _run(nc, [arrays], core_ids=[0])
    return tuple(r.results[0][f"out_{i}_dram"] for i in range(len(outs)))
```
